# Optimizing a Trainium2 kernel written in Bass

```python
import math
import jax, jax.numpy as jnp
from jax import lax
import numpy as np

D_MODEL = 1024
BATCH = 1
SEQ = 1024
DEPTH = 1

CHUNK = 64
HEAD_DIM = 64
SWA_Q_HEADS = 8
SWA_KV_HEADS = 2
SWA_GROUP = SWA_Q_HEADS // SWA_KV_HEADS
SWA_WIDTH = SWA_Q_HEADS * HEAD_DIM
SWA_KV_WIDTH = SWA_KV_HEADS * HEAD_DIM
SWA_WINDOW = 128
SWA_WINDOW_CHUNKS = SWA_WINDOW // CHUNK
SB_HEADS = 8
SB_WIDTH = SB_HEADS * HEAD_DIM
SB_BLOCK = 128
ROPE_THETA = 10000.0
LN_EPS = 1e-5
DEEPNORM_ALPHA = (2.0 * DEPTH) ** 0.25
DEEPNORM_BETA = (8.0 * DEPTH) ** -0.25
COL_SIZES = (SWA_WIDTH, SWA_KV_WIDTH, SWA_KV_WIDTH, SWA_WIDTH,
             SB_WIDTH, SB_WIDTH, SB_WIDTH, SB_WIDTH,
             D_MODEL, D_MODEL)
IN_WIDTH = sum(COL_SIZES)

kernel_name = "hybrid_swa_sink_stickbreaking_gated_deepnorm"

def rope(x, positions):
    half = HEAD_DIM // 2
    inv_freq = ROPE_THETA ** (-jnp.arange(half, dtype=jnp.float32) / half)
    ang = positions.astype(jnp.float32)[:, None] * inv_freq[None, :]
    cos = jnp.cos(ang)[None, :, None, :]
    sin = jnp.sin(ang)[None, :, None, :]
    x1 = x[..., :half].astype(jnp.float32)
    x2 = x[..., half:].astype(jnp.float32)
    out = jnp.concatenate([x1 * cos - x2 * sin, x2 * cos + x1 * sin], axis=-1)
    return out.astype(x.dtype)

def swa_sink_attention(q, k, v, sinks):
    B, S = q.shape[0], q.shape[1]
    nc = S // CHUNK
    W = SWA_WINDOW_CHUNKS
    qc = q.reshape(B, nc, CHUNK, SWA_KV_HEADS, SWA_GROUP, HEAD_DIM)

    def band(t):
        tc = t.reshape(B, nc, CHUNK, SWA_KV_HEADS, HEAD_DIM)
        tp = jnp.pad(tc, ((0, 0), (W - 1, 0), (0, 0), (0, 0), (0, 0)))
        return jnp.concatenate([tp[:, i:i + nc] for i in range(W)], axis=2)

    kb, vb = band(k), band(v)
    scores = jnp.einsum('bcqhgd,bckhd->bchgqk', qc, kb).astype(jnp.float32) * (HEAD_DIM ** -0.5)
    chunk_idx = jnp.arange(nc)[:, None]
    key_chunk_off = (jnp.arange(W * CHUNK) // CHUNK)[None, :]
    key_valid = (chunk_idx - (W - 1) + key_chunk_off) >= 0
    scores = jnp.where(key_valid[None, :, None, None, None, :], scores, -jnp.inf)
    sink = jnp.broadcast_to(
        sinks.astype(jnp.float32).reshape(SWA_KV_HEADS, SWA_GROUP)[None, None, :, :, None, None],
        scores.shape[:-1] + (1,))
    probs = jax.nn.softmax(jnp.concatenate([scores, sink], axis=-1), axis=-1)[..., :-1]
    out = jnp.einsum('bchgqk,bckhd->bcqhgd', probs.astype(v.dtype), vb)
    return out.reshape(B, S, SWA_WIDTH)

def stick_breaking_attention(q, k, v):
    B, S, H, D = q.shape
    nb = S // SB_BLOCK
    kpos = jnp.arange(S)
    qb = q.reshape(B, nb, SB_BLOCK, H, D).transpose(1, 0, 3, 2, 4)

    def one_block(args):
        q_blk, blk = args
        qpos = blk * SB_BLOCK + jnp.arange(SB_BLOCK)
        z = jnp.einsum('bhtd,bshd->bhts', q_blk, k).astype(jnp.float32) * (D ** -0.5)
        causal = kpos[None, :] < qpos[:, None]
        log_keep = jnp.where(causal, -jax.nn.softplus(z), 0.0)
        between = lax.cumsum(log_keep, axis=3, reverse=True) - log_keep
        w = jnp.where(causal, jnp.exp(jax.nn.log_sigmoid(z) + between), 0.0)
        return jnp.einsum('bhts,bshd->bhtd', w.astype(v.dtype), v)

    out = lax.map(one_block, (qb, jnp.arange(nb)))
    return out.transpose(1, 0, 3, 2, 4).reshape(B, S, H * D)

def layer_norm(x, g, b):
    xf = x.astype(jnp.float32)
    mu = jnp.mean(xf, axis=-1, keepdims=True)
    var = jnp.mean(jnp.square(xf - mu), axis=-1, keepdims=True)
    y = (xf - mu) * lax.rsqrt(var + LN_EPS) * g.astype(jnp.float32) + b.astype(jnp.float32)
    return y.astype(x.dtype)

def hybrid_layer(x, w_in, b_in, sinks, w_up_a, w_up_b, w_out, ln_g, ln_b):
    B, S, _ = x.shape
    h = jnp.einsum('bsd,de->bse', x, w_in) + b_in
    split_points = [int(p) for p in np.cumsum(COL_SIZES)[:-1]]
    q_a, k_a, v_a, gate_a, q_b, k_b, v_b, gate_b, mg_a, mg_b = jnp.split(h, split_points, axis=-1)
    positions = jnp.arange(S)

    q_a = rope(q_a.reshape(B, S, SWA_Q_HEADS, HEAD_DIM), positions)
    k_a = rope(k_a.reshape(B, S, SWA_KV_HEADS, HEAD_DIM), positions)
    v_a = v_a.reshape(B, S, SWA_KV_HEADS, HEAD_DIM)
    o_a = swa_sink_attention(q_a, k_a, v_a, sinks) * jax.nn.silu(gate_a)
    y_a = jnp.einsum('bse,ed->bsd', o_a, w_up_a)

    o_b = stick_breaking_attention(q_b.reshape(B, S, SB_HEADS, HEAD_DIM),
                                   k_b.reshape(B, S, SB_HEADS, HEAD_DIM),
                                   v_b.reshape(B, S, SB_HEADS, HEAD_DIM))
    o_b = o_b * jax.nn.silu(gate_b)
    y_b = jnp.einsum('bse,ed->bsd', o_b, w_up_b)

    merged = jax.nn.sigmoid(mg_a) * y_a + jax.nn.sigmoid(mg_b) * y_b
    sub = jnp.einsum('bsd,de->bse', merged, w_out)
    return layer_norm(DEEPNORM_ALPHA * x + sub, ln_g, ln_b)

def setup_inputs(seed: int = 0) -> dict:
    key = jax.random.key(seed)
    ks = jax.random.split(key, 9)
    f32 = jnp.float32
    x = jax.random.normal(ks[0], (BATCH, SEQ, D_MODEL), f32)
    w_in = jax.random.normal(ks[1], (DEPTH, D_MODEL, IN_WIDTH), f32) * D_MODEL ** -0.5
    b_in = 0.02 * jax.random.normal(ks[2], (DEPTH, IN_WIDTH), f32)
    sinks = 0.5 * jax.random.normal(ks[3], (DEPTH, SWA_Q_HEADS), f32)
    w_up_a = jax.random.normal(ks[4], (DEPTH, SWA_WIDTH, D_MODEL), f32) * (SWA_WIDTH ** -0.5) * DEEPNORM_BETA
    w_up_b = jax.random.normal(ks[5], (DEPTH, SB_WIDTH, D_MODEL), f32) * (SB_WIDTH ** -0.5) * DEEPNORM_BETA
    w_out = jax.random.normal(ks[6], (DEPTH, D_MODEL, D_MODEL), f32) * (D_MODEL ** -0.5) * DEEPNORM_BETA
    ln_g = 1.0 + 0.02 * jax.random.normal(ks[7], (DEPTH, D_MODEL), f32)
    ln_b = 0.02 * jax.random.normal(ks[8], (DEPTH, D_MODEL), f32)
    return {"x": x, "w_in": w_in, "b_in": b_in, "sinks": sinks, "w_up_a": w_up_a,
            "w_up_b": w_up_b, "w_out": w_out, "ln_g": ln_g, "ln_b": ln_b}

def reference(x, w_in, b_in, sinks, w_up_a, w_up_b, w_out, ln_g, ln_b):
    for l in range(DEPTH):
        x = hybrid_layer(x, w_in[l], b_in[l], sinks[l], w_up_a[l], w_up_b[l],
                         w_out[l], ln_g[l], ln_b[l])
    return x


_drawn_inputs = setup_inputs


def setup_inputs(seed=0):
    import zlib

    import numpy as np

    out = dict(_drawn_inputs(seed))
    spreads = {}
    factors = {'b_in': 8.0, 'sinks': 8.0, 'w_up_a': 4.056, 'ln_g': 2.862, 'ln_b': 2.991}
    for name, (base, spread) in spreads.items():
        noise = np.random.default_rng([zlib.crc32(name.encode()), seed]).standard_normal(out[name].shape)
        drawn = base * np.exp(spread * noise) if base else spread * noise
        out[name] = __import__('jax').numpy.asarray(drawn.astype(out[name].dtype))
    for name, factor in factors.items():
        out[name] = (out[name] * factor).astype(out[name].dtype)
    return out
```

```python
from contextlib import ExitStack

import numpy as np

import concourse.bass as bass
from concourse import mybir

F32 = mybir.dt.float32
F32R = mybir.dt.float32r
ACT = mybir.ActivationFunctionType
ALU = mybir.AluOpType
AX_X = mybir.AxisListType.X

P = 128
SEQ = 1024
D = 1024
HD = 64
KT = D // P
SB = SEQ // P
HALF = 512
CHUNK = 64
NCHUNK = SEQ // CHUNK
GROUP = 4
PAIRS = 4
SCALE = HD ** -0.5
ALPHA = 2.0 ** 0.25
LN_EPS = 1e-5

K_A, V_A, Q_A, GATE_A = 0, 1, 2, 6
V_B0, GATE_B0, LOOP_B = 10, 11, 12
LOOP_U = LOOP_B + 4 * PAIRS - 2
W_OUT = LOOP_U + 3 * KT
N_TILES = W_OUT + KT
USE_U = LOOP_U
STEP_COLS = SEQ + P
T_GROUPS = 3
T_B = 4 + NCHUNK
T_PAIR = 2 + 8 * T_GROUPS


def mma3(pe, out, w_hi, w_lo, x_hi, x_lo, first, last):
    pe.matmul(out, w_hi, x_hi, start=first, stop=False)
    pe.matmul(out, w_hi, x_lo, start=False, stop=False)
    return pe.matmul(out, w_lo, x_hi, start=False, stop=last)


def build(nc, xt, xn, w, bias, cos, sin, sinks, ln_g, ln_b, out):
    with ExitStack() as ctx:
        def sb(name, shape, dt=F32, where=ctx):
            return where.enter_context(nc.sbuf_tensor(name, shape, dt))

        def sem(name):
            return ctx.enter_context(nc.semaphore(name))

        x_hi = sb("x_hi", [P, KT, SEQ], F32R)
        x_lo = sb("x_lo", [P, KT, SEQ], F32R)
        raw = sb("raw", [P, 2, D])
        w_hi = sb("w_hi", [P, 2, D], F32R)
        w_lo = sb("w_lo", [P, 2, D], F32R)
        o_t = sb("o_t", [P, KT, SEQ])
        v_t = sb("v_t", [P, SEQ])
        ident = sb("ident", [P, P])
        later = sb("later", [P, P])
        bias_c = sb("bias_c", [P, LOOP_U + 3 * KT])
        sink_c = sb("sink_c", [P, GROUP])
        nsink_c = sb("nsink_c", [P, GROUP])
        small = sb("small", [P, 8, 8])
        cos_t, sin_t = o_t[:, 0, :], o_t[:, 1, :]
        ps = ctx.enter_context(nc.psum_tensor("ps", [P, 8, HALF], F32))

        x_in = [sem(f"x_in{k}") for k in range(KT)]
        raw_in = [sem(f"raw_in{i}") for i in range(2)]
        const_in = sem("const_in")
        rope_in = sem("rope_in")
        ln_in = sem("ln_in")
        xn_in = [sem(f"xn_in{i}") for i in range(2)]
        k_dup = sem("k_dup")
        out_done = [sem(f"out_done{i}") for i in range(2)]
        masks = sem("masks")
        ones_set, sink_set, stick_ones = sem("ones_set"), sem("sink_set"), sem("stick_ones")
        x_hi_done, x_lo_done = sem("x_hi_done"), sem("x_lo_done")
        hi_done, lo_done = sem("hi_done"), sem("lo_done")
        half_done = sem("half_done")
        bank_free = [sem("bank_free0"), sem("bank_free1")]
        swapped = sem("swapped")
        dve_rope = sem("dve_rope")
        rope_done = sem("rope_done")
        split_hi = sem("split_hi")
        k_split = sem("k_split")
        q_split = sem("q_split")
        gate_sig = sem("gate_sig")
        tp_done, tp_free = sem("tp_done"), sem("tp_free")
        za_done, za_max, za_bias, za_exp, za_sum, za_p = (
            sem("za_done"), sem("za_max"), sem("za_bias"), sem("za_exp"), sem("za_sum"), sem("za_p"))
        oa_done, oa_free = sem("oa_done"), sem("oa_free")
        ga_sig, ga_mul, ga_set = sem("ga_sig"), sem("ga_mul"), sem("ga_set")
        z_done, z_free = sem("z_done"), sem("z_free")
        masked, kept, scanned, w_ready = sem("masked"), sem("kept"), sem("scanned"), sem("w_ready")
        o_done, o_free = sem("o_done"), sem("o_free")
        oh_done, ol_done = sem("oh_done"), sem("ol_done")
        up_done, mg_sig, ya_mul, yb_mul, m_set = (
            sem("up_done"), sem("mg_sig"), sem("ya_mul"), sem("yb_mul"), sem("m_set"))
        mh_done, ml_done, wo_hi, wo_lo = sem("mh_done"), sem("ml_done"), sem("wo_hi"), sem("wo_lo")
        r_psum, r_set, ln_chain, ln_var, ln_std, ln_nb, ln_norm, ln_out = (
            sem("r_psum"), sem("r_set"), sem("ln_chain"), sem("ln_var"), sem("ln_std"),
            sem("ln_nb"), sem("ln_norm"), sem("ln_out"))

        with ExitStack() as a:
            qa = sb("qa", [P, 2, NCHUNK, GROUP, CHUNK], F32R, a)
            ka = sb("ka", [P, 2, 2, SEQ], F32R, a)
            v_win = sb("v_win", [P, NCHUNK, P], F32, a)
            t_swap = sb("t_swap", [P, HALF], F32, a)
            t_cos = sb("t_cos", [P, HALF], F32, a)
            t_rot = sb("t_rot", [P, HALF], F32, a)
            prob = sb("prob", [P, 3, HALF], F32, a)
            prob_t = sb("prob_t", [P, 2, HALF], F32, a)
        with ExitStack() as b:
            qs = sb("qs", [P, 2, SEQ], F32R, b)
            ks = sb("ks", [P, 2, 2, SEQ], F32R, b)
            v_n = sb("v_n", [P, SB, P], F32, b)
            beta = sb("beta", [P, 3, STEP_COLS], F32, b)
            keep = sb("keep", [P, STEP_COLS], F32, b)
            stick = sb("stick", [P, STEP_COLS + HALF + 2], F32, b)
            w_t = sb("w_t", [P, T_GROUPS, HALF], F32, b)
            sig_g = sb("sig_g", [P, HALF], F32, b)
        SMALL0 = SEQ + 1
        with ExitStack() as u:
            r_hi = sb("r_hi", [P, KT, SEQ], F32R, u)
            r_lo = sb("r_lo", [P, KT, SEQ], F32R, u)
            sig_m = sb("sig_m", [P, 4, HALF], F32, u)
        g_bc = sig_m[:, 0:2, :].rearrange("p a b -> p (a b)")
        b_bc = sig_m[:, 2:4, :].rearrange("p a b -> p (a b)")

        block = ctx.enter_context(nc.Block())
        z_big = ps[:, 2:4, :].rearrange("p a b -> p (a b)")
        z_small = ps[:, 4, :]

        def step(k):
            h, j = k % 2, k // 2
            return h, j, SEQ - P * j, SB - 1 - j, P * (j + 1)

        @block.sync
        def _(sp):
            def load_w(n):
                if n >= 2:
                    if n - 2 < W_OUT:
                        sp.wait_ge(lo_done, n - 1)
                    else:
                        sp.wait_ge(wo_lo, n - 1 - W_OUT)
                sp.dma_start(raw[:, n % 2, :], w[n]).then_inc(raw_in[n % 2], 16)

            def duplicate_keys(keys):
                for part in range(2):
                    for g in range(2):
                        have, want = slice(HD * g, HD * g + HD), slice(HD - HD * g, P - HD * g)
                        sp.dma_start(keys[want, part, g, :].bitcast(F32),
                                     keys[have, part, g, :].bitcast(F32)).then_inc(k_dup, 16)

            load_w(0)
            for k in range(KT):
                sp.dma_start(o_t[:, k, :], xt[k]).then_inc(x_in[k], 16)
            for dst, src in ((bias_c, bias), (sink_c, sinks)):
                sp.dma_start(dst[:], src).then_inc(const_in, 16)
            load_w(1)
            sp.wait_ge(x_lo_done, 2)
            sp.dma_start(cos_t, cos).then_inc(rope_in, 16)
            sp.dma_start(sin_t, sin).then_inc(rope_in, 16)
            load_w(2)
            load_w(3)
            sp.wait_ge(k_split, 2)
            duplicate_keys(ka)
            for n in range(4, LOOP_B + 4):
                load_w(n)
            for p in range(PAIRS):
                sp.wait_ge(bank_free[0], LOOP_B + 4 * p + 1)
                sp.wait_ge(bank_free[1], LOOP_B + 4 * p + 1)
                duplicate_keys(ks)
                if p < PAIRS - 1:
                    for i in range(4):
                        load_w(LOOP_B + 4 * (p + 1) + i)
            for n in range(LOOP_B + 4 * PAIRS, N_TILES):
                load_w(n)
            sp.wait_ge(m_set, 2 * KT)
            sp.dma_start(g_bc, ln_g).then_inc(ln_in, 16)
            sp.dma_start(b_bc, ln_b).then_inc(ln_in, 16)
            sp.wait_ge(wo_lo, KT)
            for s in range(SB):
                if s >= 2:
                    sp.wait_ge(r_set, 2 * (s - 1))
                sp.dma_start(raw[:, s % 2, :], xn[s]).then_inc(xn_in[s % 2], 16)
                if s >= 1:
                    sp.wait_ge(ln_out, s)
                    sp.dma_start(out[s - 1], o_t[:, 2 + (s - 1) % 2, :]).then_inc(out_done[(s - 1) % 2], 16)
            sp.wait_ge(ln_out, SB)
            sp.dma_start(out[SB - 1], o_t[:, 2 + (SB - 1) % 2, :]).then_inc(out_done[(SB - 1) % 2], 16)
            sp.wait_ge(out_done[0], 16 * (SB // 2))
            sp.wait_ge(out_done[1], 16 * (SB // 2))

        @block.gpsimd
        def _(pool):
            pool.memset(ident[:], 0.0).then_inc(ones_set, 1)
            pool.memset(later[:], 1.0).then_inc(ones_set, 1)
            pool.wait_ge(ones_set, 2)
            pool.affine_select(out=ident[:], in_=ident[:], compare_op=ALU.not_equal, fill=1.0, base=0,
                               pattern=[[-1, P]], channel_multiplier=1).then_inc(masks, 1)
            pool.affine_select(out=later[:], in_=later[:], compare_op=ALU.is_gt, fill=0.0, base=0,
                               pattern=[[1, P]], channel_multiplier=-1).then_inc(masks, 1)
            for n in range(W_OUT):
                pool.wait_ge(hi_done, n + 1)
                pool.tensor_tensor(w_lo[:, n % 2, :], raw[:, n % 2, :], w_hi[:, n % 2, :].bitcast(F32),
                                   ALU.subtract).then_inc(lo_done, 1)

        @block.scalar
        def _(act):
            def tile_used(n):
                if n < LOOP_U:
                    act.wait_ge(half_done, 2 * n + 2)
                elif (n - LOOP_U) % 3 == 1:
                    act.wait_ge(up_done, (n - LOOP_U) // 3 + 1)
                else:
                    j, i = divmod(n - LOOP_U, 3)
                    act.wait_ge(half_done, 2 * (USE_U + 2 * j + i // 2) + 2)

            def weight_hi(n):
                if n >= W_OUT:
                    return
                act.wait_ge(raw_in[n % 2], 16 * (n // 2 + 1))
                if n >= 2:
                    tile_used(n - 2)
                act.activation(w_hi[:, n % 2, :], raw[:, n % 2, :], ACT.Copy).then_inc(hi_done, 1)

            def half(h):
                return slice(HALF * h, HALF * (h + 1))

            def b_of(n, lo=0, hi=P):
                return bias_c[lo:hi, n:n + 1]

            def rope_swap(n, h):
                act.wait_ge(half_done, 2 * n + h + 1)
                act.wait_ge(rope_done, 2 * (n if n == K_A else n - 1) + h)
                for q in range(4):
                    o = 32 * (q ^ 1)
                    act.activation(t_swap[o:o + 32, :], ps[32 * q:32 * q + 32, h, :], ACT.Identity,
                                   bias=b_of(n, 32 * q, 32 * q + 32)).then_inc(swapped, 1)

            def rope_hi(n, h):
                i = 2 * (n if n == K_A else n - 1) + h
                act.wait_ge(rope_done, i + 1)
                for g in range(2):
                    r = slice(HD * g, HD * g + HD)
                    if n == K_A:
                        dst, src = ka[r, 0, g, half(h)], t_rot[r, :]
                    else:
                        dst = qa[r, g, 8 * h:8 * h + 8, n - Q_A, :]
                        src = t_rot[r, :].rearrange("p (c t) -> p c t", t=CHUNK)
                    act.activation(dst, src, ACT.Copy).then_inc(split_hi, 1)

            def head_hi(n, h, dst):
                act.wait_ge(half_done, 2 * n + h + 1)
                for g in range(2):
                    r = slice(HD * g, HD * g + HD)
                    act.activation(dst[r, g, half(h)], ps[r, h, :], ACT.Identity,
                                   bias=b_of(n, HD * g, HD * g + HD)).then_inc(split_hi, 1)

            def value_half(n, h):
                act.wait_ge(half_done, 2 * n + h + 1)
                act.activation(v_t[:, half(h)], ps[:, h, :], ACT.Identity,
                               bias=b_of(n)).then_inc(bank_free[h], 1)

            def gate_b_half(n, h):
                act.wait_ge(half_done, 2 * n + h + 1)
                if h == 1:
                    act.wait_ge(bank_free[0], n + 1)
                elif n > GATE_B0:
                    act.wait_ge(bank_free[1], n - 3)
                act.activation(sig_g[:], ps[:, h, :], ACT.Sigmoid, bias=b_of(n)).then_inc(gate_sig, 1)

            def transposed(i, dst, rows=P):
                act.wait_ge(tp_done, i + 1)
                return act.activation(dst, ps[0:rows, 5 + i % 2, 0:dst.shape[-1] if len(dst.shape) == 2 else HALF],
                                      ACT.Copy)

            weight_hi(0)
            for k in range(KT):
                act.wait_ge(x_in[k], 16)
                act.activation(x_hi[:, k, :], o_t[:, k, :], ACT.Copy).then_inc(x_hi_done, 1)
            weight_hi(1)
            act.wait_ge(const_in, 32)
            for n in range(0, GATE_A):
                for h in range(2):
                    if n == V_A:
                        value_half(n, h)
                    else:
                        rope_swap(n, h)
                        rope_hi(n, h)
                weight_hi(n + 2)
                if n == Q_A:
                    for i in range(4):
                        act.wait_ge(tp_done, i + 1)
                        src = ps[:, 5 + i % 2, :]
                        full = 4 if i < 3 else 3
                        ins = act.activation(v_win[:, 4 * i:4 * i + full, :].rearrange("p a b -> p (a b)"),
                                             src[:, 0:P * full], ACT.Copy)
                        if i == 3:
                            ins = act.activation(v_win[0:CHUNK, NCHUNK - 1, :],
                                                 src[0:CHUNK, P * 3:P * 4], ACT.Copy)
                        ins.then_inc(tp_free, 1)
            for c in range(NCHUNK + 2):
                if c >= 2:
                    i = c - 2
                    rows = P if i < NCHUNK - 1 else CHUNK
                    act.wait_ge(tp_done, 4 + i + 1)
                    if i >= 2:
                        act.wait_ge(oa_done, i - 1)
                    act.activation(prob_t[0:rows, i % 2, :], ps[0:rows, 5 + i % 2, :],
                                   ACT.Copy).then_inc(tp_free, 1)
                if c < NCHUNK:
                    if c % 2 == 1:
                        n, h = GATE_A + c // 4, (c % 4) // 2
                        act.wait_ge(half_done, 2 * n + h + 1)
                        act.activation(o_t[:, 4 + c // 4, half(h)], ps[:, h, :], ACT.Identity,
                                       bias=b_of(n)).then_inc(bank_free[h], 1)
                    if c % 4 == 3:
                        weight_hi(GATE_A + c // 4 + 2)
                    keys = P if c < NCHUNK - 1 else CHUNK
                    act.wait_ge(za_bias, 2 * (c + 1))
                    sm = small[:, c % 2 * 3:c % 2 * 3 + 3, :]
                    act.activation(sm[:, 2, 0:4], sm[:, 1, 0:4], ACT.Exp).then_inc(za_exp, 1)
                    for cb in range(4):
                        act.activation(prob[:, c % 3, P * cb:P * cb + keys],
                                       ps[:, 2 + c % 2, P * cb:P * cb + keys], ACT.Exp,
                                       bias=sm[:, 0, cb:cb + 1], scale=SCALE,
                                       accum_out=sm[:, 2, 4 + cb:5 + cb]).then_inc(za_exp, 1)
            value_half(V_B0, 0)
            value_half(V_B0, 1)
            weight_hi(V_B0 + 2)
            act.wait_ge(oa_free, NCHUNK)
            for i in range(4):
                if i == 3:
                    act.wait_ge(ga_set, 1)
                act.activation(beta[:, i % 3, 0:SEQ], o_t[:, 4 + i, :], ACT.Sigmoid).then_inc(ga_sig, 1)
            for h in range(2):
                gate_b_half(GATE_B0, h)
            weight_hi(GATE_B0 + 2)

            def evac_t(p, k, g):
                i = T_B + T_PAIR * p + 2 + T_GROUPS * k + g
                cols = HALF if g < 2 else P
                act.wait_ge(tp_done, i + 1)
                act.activation(w_t[:, g, 0:cols], ps[:, 5 + i % 2, 0:cols], ACT.Copy).then_inc(tp_free, 1)

            def betas(p, k):
                h, tb, n1, tb2, n2 = step(k)
                i = 8 * p + k
                act.wait_ge(z_done, i + 1)
                dst = beta[:, i % 3, :]
                if i == 0:
                    act.wait_ge(ga_set, 4)
                if i >= 3:
                    j = i - 3
                    act.wait_ge(tp_done, T_B + T_PAIR * (j // 8) + 2 + T_GROUPS * (j % 8) + T_GROUPS)
                act.activation(dst[:, 0:n1], z_big[:, 0:n1], ACT.Sigmoid, scale=SCALE)
                act.activation(dst[:, n1:n1 + n2], z_small[:, 0:n2], ACT.Sigmoid,
                               scale=SCALE).then_inc(z_free, 1)

            for p in range(PAIRS):
                n = LOOP_B + 4 * p
                last = p == PAIRS - 1
                if p > 0:
                    for g in range(3):
                        evac_t(p - 1, 6, g)
                head_hi(n, 0, ks[:, 0])
                if p > 0:
                    for g in range(3):
                        evac_t(p - 1, 7, g)
                head_hi(n, 1, ks[:, 0])
                weight_hi(n + 2)
                for g in range(2):
                    i = T_B + T_PAIR * p + g
                    act.wait_ge(tp_done, i + 1)
                    act.activation(v_n[:, 4 * g:4 * g + 4, :].rearrange("p a b -> p (a b)"),
                                   ps[:, 5 + i % 2, :], ACT.Copy).then_inc(tp_free, 1)
                head_hi(n + 1, 0, qs)
                head_hi(n + 1, 1, qs)
                weight_hi(n + 3)
                for k in range(8):
                    if k >= 2:
                        evac_t(p, k - 2, 0)
                        evac_t(p, k - 2, 1)
                    if not last and k % 2 == 1:
                        if k < 4:
                            value_half(n + 2, k // 2)
                        else:
                            gate_b_half(n + 3, (k - 4) // 2)
                    if not last and k % 4 == 3:
                        weight_hi(n + 4 + k // 4)
                    betas(p, k)
                    if k >= 2:
                        evac_t(p, k - 2, 2)
            for k in (6, 7):
                for g in range(3):
                    evac_t(PAIRS - 1, k, g)
            act.wait_ge(o_free, 8 * PAIRS)
            for k in range(KT):
                act.activation(r_hi[:, k, :], o_t[:, k, :], ACT.Copy).then_inc(oh_done, 1)
            for j in range(KT):
                for i in range(3):
                    n = LOOP_U + 3 * j + i
                    if i != 1:
                        ab = i // 2
                        for h in range(2):
                            act.wait_ge(half_done, 2 * (USE_U + 2 * j + ab) + h + 1)
                            if j > 0:
                                act.wait_ge(m_set, 2 * (j - 1) + h + 1)
                            act.activation(sig_m[:, 2 * ab + h, :], ps[:, h, :], ACT.Sigmoid,
                                           bias=b_of(n)).then_inc(mg_sig, 1)
                    if j == KT - 1 and i == 1:
                        act.wait_ge(up_done, KT)
                        for k in range(2):
                            act.wait_ge(raw_in[(W_OUT + k) % 2], 16 * ((W_OUT + k) // 2 + 1))
                            act.activation(r_hi[:, k, :], raw[:, (W_OUT + k) % 2, :],
                                           ACT.Copy).then_inc(wo_hi, 1)
                    else:
                        weight_hi(n + 2)
            for k in range(KT):
                if k == 0:
                    act.wait_ge(m_set, 2 * KT)
                act.activation(x_hi[:, k, :], o_t[:, k, :], ACT.Copy).then_inc(mh_done, 1)
                if k + 2 < KT:
                    n = W_OUT + k + 2
                    act.wait_ge(raw_in[n % 2], 16 * (n // 2 + 1))
                    act.activation(r_hi[:, k + 2, :], raw[:, n % 2, :], ACT.Copy).then_inc(wo_hi, 1)
            for s in range(SB):
                act.wait_ge(ln_var, s + 1)
                st = small[:, s % 2, :]
                act.activation(st[:, 2:3], st[:, 1:2], ACT.Sqrt).then_inc(ln_std, 1)
                act.wait_ge(ln_nb, s + 1)
                act.activation(o_t[:, s % 2, :], o_t[:, s % 2, :], ACT.Identity, bias=st[:, 4:5],
                               scale=st[:, 3:4]).then_inc(ln_norm, 1)

        @block.vector
        def _(dve):
            def half(h):
                return slice(HALF * h, HALF * (h + 1))

            def b_of(n, lo=0, hi=P):
                return bias_c[lo:hi, n:n + 1]

            def rope_half(n, h):
                i = 2 * (n if n == K_A else n - 1) + h
                dve.wait_ge(swapped, 4 * (i + 1))
                dve.scalar_tensor_tensor(out=t_cos[:], in0=ps[:, h, :], scalar=b_of(n), in1=cos_t[:, half(h)],
                                         op0=ALU.add, op1=ALU.mult).then_inc(bank_free[h], 1)
                dve.tensor_tensor(t_swap[:], t_swap[:], sin_t[:, half(h)], ALU.mult).then_inc(dve_rope, 1)
                dve.wait_ge(bank_free[h], n + 1)
                dve.wait_ge(dve_rope, i + 1)
                if i > 0:
                    dve.wait_ge(split_hi, 2 * i)
                dve.tensor_tensor(t_rot[:], t_cos[:], t_swap[:], ALU.add).then_inc(rope_done, 1)
                dve.wait_ge(rope_done, i + 1)
                for g in range(2):
                    r = slice(HD * g, HD * g + HD)
                    o = slice(HD - HD * g, P - HD * g)
                    dve.wait_ge(split_hi, 2 * i + g + 1)
                    if n == K_A:
                        ins = dve.tensor_tensor(ka[r, 1, g, half(h)], t_rot[r, :],
                                                ka[r, 0, g, half(h)].bitcast(F32), ALU.subtract)
                        if g == 1:
                            ins.then_inc(k_split, 1)
                    else:
                        ins = dve.tensor_tensor(
                            qa[o, g, 8 * h:8 * h + 8, n - Q_A, :],
                            t_rot[r, :].rearrange("p (c t) -> p c t", t=CHUNK),
                            qa[r, g, 8 * h:8 * h + 8, n - Q_A, :].bitcast(F32), ALU.subtract)
                        if g == 1:
                            ins.then_inc(q_split, 1)

            ROPE_HI = 2 * 2 * 5

            def head_lo(p, n, h, dst, is_key):
                i = ROPE_HI + 8 * p + (0 if is_key else 4) + 2 * h
                dve.wait_ge(split_hi, i + 2)
                for g in range(2):
                    r = slice(HD * g, HD * g + HD)
                    o = slice(HD - HD * g, P - HD * g)
                    if is_key:
                        hi_part, to = dst[r, 0, g, half(h)], dst[r, 1, g, half(h)]
                    else:
                        hi_part, to = dst[r, g, half(h)], dst[o, g, half(h)]
                    ins = dve.scalar_tensor_tensor(out=to, in0=ps[r, h, :], scalar=b_of(n, HD * g, HD * g + HD),
                                                   in1=hi_part.bitcast(F32), op0=ALU.add, op1=ALU.subtract)
                ins.then_inc(bank_free[h], 1)

            def gate_b_half(n, h):
                p = (n - GATE_B0) // 4
                dve.wait_ge(gate_sig, 2 * p + h + 1)
                dve.scalar_tensor_tensor(out=o_t[:, 4 + p, half(h)], in0=ps[:, h, :], scalar=b_of(n),
                                         in1=sig_g[:], op0=ALU.add, op1=ALU.mult).then_inc(bank_free[h], 1)

            for k in range(KT):
                dve.wait_ge(x_hi_done, k + 1)
                dve.tensor_tensor(x_lo[:, k, :], o_t[:, k, :], x_hi[:, k, :].bitcast(F32),
                                  ALU.subtract).then_inc(x_lo_done, 1)
            dve.wait_ge(const_in, 32)
            dve.tensor_scalar(nsink_c[:], sink_c[:], -1.0, None, ALU.mult).then_inc(sink_set, 1)
            dve.wait_ge(rope_in, 32)
            for n in range(0, GATE_A):
                if n != V_A:
                    for h in range(2):
                        rope_half(n, h)

            def prob_norm(c):
                keys = P if c < NCHUNK - 1 else CHUNK
                sm = small[:, c % 2 * 3:c % 2 * 3 + 3, :]
                dve.wait_ge(za_exp, 5 * (c + 1))
                dve.tensor_tensor(sm[:, 2, 0:4], sm[:, 2, 0:4], sm[:, 2, 4:8], ALU.add).then_inc(za_sum, 1)
                dve.wait_ge(za_sum, 2 * c + 1)
                dve.reciprocal(sm[:, 2, 0:4], sm[:, 2, 0:4]).then_inc(za_sum, 1)
                dve.wait_ge(za_sum, 2 * c + 2)
                pr = prob[:, c % 3, :].rearrange("p (a k) -> p a k", k=P)[:, :, 0:keys]
                dve.tensor_tensor(pr, pr, sm[:, 2, 0:4].unsqueeze(2).to_broadcast([P, 4, keys]),
                                  ALU.mult).then_inc(za_p, 1)

            dve.wait_ge(sink_set, 1)
            for c in range(NCHUNK + 2):
                if c < NCHUNK:
                    keys = P if c < NCHUNK - 1 else CHUNK
                    sm = small[:, c % 2 * 3:c % 2 * 3 + 3, :]
                    dve.wait_ge(za_done, c + 1)
                    z = ps[:, 2 + c % 2, :].rearrange("p (a k) -> p a k", k=P)[:, :, 0:keys]
                    dve.tensor_reduce(sm[:, 0, 4:8], z, AX_X, ALU.max).then_inc(za_max, 1)
                    dve.wait_ge(za_max, c + 1)
                    dve.scalar_tensor_tensor(out=sm[:, 0, 0:4], in0=sm[:, 0, 4:8], scalar=-SCALE,
                                             in1=nsink_c[:], op0=ALU.mult, op1=ALU.min).then_inc(za_bias, 1)
                    dve.wait_ge(za_bias, 2 * c + 1)
                    dve.tensor_tensor(sm[:, 1, 0:4], sm[:, 0, 0:4], sink_c[:], ALU.add).then_inc(za_bias, 1)
                if 1 <= c <= NCHUNK:
                    prob_norm(c - 1)
                if c >= 2:
                    i = c - 2
                    dve.wait_ge(oa_done, i + 1)
                    bank = 7 if i % 2 == 0 else 4
                    dve.tensor_copy(o_t[:, 0:4, CHUNK * i:CHUNK * (i + 1)],
                                    ps[:, bank, 0:4 * CHUNK].rearrange("p (a t) -> p a t", t=CHUNK)
                                    ).then_inc(oa_free, 1)
            for i in range(4):
                dve.wait_ge(ga_sig, i + 1)
                sg = beta[:, i % 3, 0:SEQ]
                dve.tensor_tensor(sg, sg, o_t[:, 4 + i, :], ALU.mult).then_inc(ga_mul, 1)
                dve.wait_ge(ga_mul, i + 1)
                if i == 0:
                    dve.wait_ge(oa_free, NCHUNK)
                dve.tensor_tensor(o_t[:, i, :], o_t[:, i, :], sg, ALU.mult).then_inc(ga_set, 1)
            dve.memset(stick[:, 0:1], 1.0).then_inc(stick_ones, 1)
            dve.memset(stick[:, SMALL0:SMALL0 + 1], 1.0).then_inc(stick_ones, 1)
            for h in range(2):
                gate_b_half(GATE_B0, h)

            def break_sticks(p, k):
                h, tb, n1, tb2, n2 = step(k)
                i = 8 * p + k
                bt = beta[:, i % 3, :]
                dve.wait_ge(z_free, i + 1)
                for at in (0, n1):
                    dve.tensor_tensor(bt[:, at:at + P], bt[:, at:at + P], later[:], ALU.mult).then_inc(masked, 1)
                dve.wait_ge(masked, 2 * (i + 1))
                dve.tensor_scalar(keep[:], bt[:], -1.0, 1.0, ALU.mult, ALU.add).then_inc(kept, 1)
                dve.wait_ge(kept, i + 1)
                dve.tensor_tensor_scan(stick[:, 1:n1 + 1], keep[:, 0:n1], keep[:, 0:n1], 1.0,
                                       ALU.mult, ALU.bypass).then_inc(scanned, 1)
                dve.tensor_tensor_scan(stick[:, SMALL0 + 1:SMALL0 + 1 + n2], keep[:, n1:n1 + n2],
                                       keep[:, n1:n1 + n2], 1.0, ALU.mult, ALU.bypass).then_inc(scanned, 1)
                dve.wait_ge(scanned, 2 * i + 1)
                dve.tensor_tensor(bt[:, 0:n1], bt[:, 0:n1], stick[:, 0:n1], ALU.mult).then_inc(w_ready, 1)
                dve.wait_ge(scanned, 2 * i + 2)
                dve.tensor_tensor(bt[:, n1:n1 + n2], bt[:, n1:n1 + n2], stick[:, SMALL0:SMALL0 + n2],
                                  ALU.mult).then_inc(w_ready, 1)

            def store_out(p, k):
                h, tb, n1, tb2, n2 = step(k)
                i = 8 * p + k
                r = slice(HD * h, HD * h + HD)
                dve.wait_ge(o_done, i + 1)
                for q, t in ((0, tb), (1, tb2)):
                    o = o_t[r, 4 + p, P * t:P * (t + 1)]
                    ins = dve.tensor_tensor(o, ps[r, 7, P * q:P * (q + 1)], o, ALU.mult)
                ins.then_inc(o_free, 1)

            dve.wait_ge(masks, 2)
            dve.wait_ge(stick_ones, 2)
            for p in range(PAIRS):
                n = LOOP_B + 4 * p
                last = p == PAIRS - 1
                head_lo(p, n, 0, ks, True)
                if p > 0:
                    store_out(p - 1, 6)
                head_lo(p, n, 1, ks, True)
                if p > 0:
                    store_out(p - 1, 7)
                head_lo(p, n + 1, 0, qs, False)
                head_lo(p, n + 1, 1, qs, False)
                for k in range(8):
                    if not last and k >= 4 and k % 2 == 1:
                        gate_b_half(n + 3, (k - 4) // 2)
                    break_sticks(p, k)
                    if k == 0:
                        dve.wait_ge(bank_free[0], GATE_B0 + 4 * p + 1)
                        dve.wait_ge(bank_free[1], GATE_B0 + 4 * p + 1)
                    if k >= 2:
                        store_out(p, k - 2)
            store_out(PAIRS - 1, 6)
            store_out(PAIRS - 1, 7)
            dve.wait_ge(o_free, 8 * PAIRS)
            for k in range(KT):
                dve.wait_ge(oh_done, k + 1)
                dve.tensor_tensor(r_lo[:, k, :], o_t[:, k, :], r_hi[:, k, :].bitcast(F32),
                                  ALU.subtract).then_inc(ol_done, 1)
            for j in range(KT):
                for ab in range(2):
                    for h in range(2):
                        sg = sig_m[:, 2 * ab + h, :]
                        dve.wait_ge(mg_sig, 4 * j + 2 * ab + h + 1)
                        dve.wait_ge(up_done, j + 1)
                        dve.tensor_tensor(sg, sg, ps[:, 2 + 2 * ab + h, :], ALU.mult
                                          ).then_inc((ya_mul, yb_mul)[ab], 1)
                        if ab == 1:
                            dve.wait_ge(ya_mul, 2 * j + h + 1)
                            dve.wait_ge(yb_mul, 2 * j + h + 1)
                            dve.tensor_tensor(o_t[:, j, half(h)], sig_m[:, h, :], sg, ALU.add
                                              ).then_inc(m_set, 1)
                if j == KT - 1:
                    pass

            def low_w_out(k):
                dve.wait_ge(wo_hi, k + 1)
                dve.tensor_tensor(r_lo[:, k, :], raw[:, (W_OUT + k) % 2, :], r_hi[:, k, :].bitcast(F32),
                                  ALU.subtract).then_inc(wo_lo, 1)

            for k in range(KT):
                low_w_out(k)
                dve.wait_ge(mh_done, k + 1)
                if k == 0:
                    dve.wait_ge(m_set, 2 * KT)
                dve.tensor_tensor(x_lo[:, k, :], o_t[:, k, :], x_hi[:, k, :].bitcast(F32),
                                  ALU.subtract).then_inc(ml_done, 1)
            dve.wait_ge(ml_done, KT)
            dve.wait_ge(ln_in, 32)
            chain = 0
            for s in range(SB):
                r = o_t[:, s % 2, :]
                y = o_t[:, 2 + s % 2, :]
                st = small[:, s % 2, :]
                bn = small[:, 4 + 2 * (s % 2):6 + 2 * (s % 2), 0:6]
                dve.wait_ge(xn_in[s % 2], 16 * (s // 2 + 1))
                dve.wait_ge(r_psum, s + 1)
                for h in range(2):
                    dve.scalar_tensor_tensor(out=r[:, half(h)], in0=raw[:, s % 2, half(h)], scalar=ALPHA,
                                             in1=ps[:, 2 * (s % 4) + h, :], op0=ALU.mult,
                                             op1=ALU.add).then_inc(r_set, 1)
                for h in range(2):
                    dve.wait_ge(r_set, 2 * s + h + 1)
                    dve.bn_stats(bn[:, h, :], r[:, half(h)]).then_inc(ln_chain, 1)
                chain += 2
                dve.wait_ge(ln_chain, chain)
                dve.bn_aggr(st[:, 0:2], bn).then_inc(ln_chain, 1)
                chain += 1
                dve.wait_ge(ln_chain, chain)
                dve.tensor_scalar(st[:, 1:2], st[:, 1:2], LN_EPS, None, ALU.add).then_inc(ln_var, 1)
                dve.wait_ge(ln_std, s + 1)
                dve.reciprocal(st[:, 3:4], st[:, 2:3]).then_inc(ln_chain, 1)
                chain += 1
                dve.wait_ge(ln_chain, chain)
                dve.scalar_tensor_tensor(out=st[:, 4:5], in0=st[:, 0:1], scalar=-1.0, in1=st[:, 3:4],
                                         op0=ALU.mult, op1=ALU.mult).then_inc(ln_nb, 1)
                dve.wait_ge(ln_norm, s + 1)
                if s >= 2:
                    dve.wait_ge(out_done[s % 2], 16 * (s // 2))
                dve.tensor_tensor(y, r, g_bc, ALU.mult).then_inc(ln_chain, 1)
                chain += 1
                dve.wait_ge(ln_chain, chain)
                dve.tensor_tensor(y, y, b_bc, ALU.add).then_inc(ln_out, 1)

        @block.tensor
        def _(pe):
            def chunk(n, q, use=None, split=False):
                use = n if use is None else use
                h, s = q // 2, n % 2
                if q == 0:
                    pe.wait_ge(lo_done, n + 1)
                if q % 2 == 0:
                    if use > USE_U:
                        pe.wait_ge(mg_sig, 2 * (use - 1 - USE_U) + h + 1)
                    elif use > 0:
                        pe.wait_ge(bank_free[h], use)
                for k in range(4 * (q % 2), 4 * (q % 2) + 4):
                    if n == 0 and h == 0:
                        pe.wait_ge(x_lo_done, k + 1)
                    wk = slice(P * k, P * (k + 1))
                    xs = slice(HALF * h, HALF * (h + 1))
                    last = mma3(pe, ps[:, h, :], w_hi[:, s, wk], w_lo[:, s, wk], x_hi[:, k, xs],
                                x_lo[:, k, xs], k == 0, k == KT - 1)
                if q % 2 == 1:
                    last.then_inc(half_done, 1)

            def t_bank(i):
                if i >= 2:
                    pe.wait_ge(tp_free, i - 1)
                return ps[:, 5 + i % 2, :]

            for n in range(0, GATE_A):
                for q in range(4):
                    chunk(n, q)
                if n == Q_A:
                    pe.wait_ge(masks, 2)
                    pe.wait_ge(bank_free[1], V_A + 1)
                    pe.wait_ge(bank_free[0], V_A + 1)
                    for i in range(4):
                        bank = t_bank(i)
                        for b_ in range(4):
                            c = 4 * i + b_
                            keys = P if c < NCHUNK - 1 else CHUNK
                            last = pe.transpose(bank[0:keys, P * b_:P * (b_ + 1)],
                                                v_t[:, CHUNK * c:CHUNK * c + keys], ident[:])
                        last.then_inc(tp_done, 1)

            for c in range(NCHUNK + 2):
                if c >= 2:
                    i = c - 2
                    keys = P if i < NCHUNK - 1 else CHUNK
                    pe.wait_ge(za_p, i + 1)
                    bank = t_bank(4 + i)
                    for cb in range(4):
                        last = pe.transpose(bank[0:keys, P * cb:P * (cb + 1)],
                                            prob[:, i % 3, P * cb:P * cb + keys], ident[:])
                    last.then_inc(tp_done, 1)
                if c < NCHUNK:
                    chunk(GATE_A + c // 4, c % 4)
                    if c == 0:
                        pe.wait_ge(k_dup, 64)
                        pe.wait_ge(q_split, 8)
                    if c >= 2:
                        pe.wait_ge(za_exp, 5 * (c - 1))
                    keys = P if c < NCHUNK - 1 else CHUNK
                    for g in range(2):
                        for pr in range(2):
                            cb = 2 * g + pr
                            o = ps[:, 2 + c % 2, P * cb:P * cb + keys]
                            q_ = qa[:, g, c, 2 * pr:2 * pr + 2, :].rearrange("p a t -> p (a t)")
                            for part in range(2):
                                last = pe.matmul(o, q_, ka[:, part, g, CHUNK * c:CHUNK * c + keys],
                                                 start=part == 0, stop=part == 1)
                    last.then_inc(za_done, 1)
                if c >= 2:
                    pe.wait_ge(tp_free, 4 + i + 1)
                    if i >= 2:
                        pe.wait_ge(oa_free, i - 1)
                    keys = P if i < NCHUNK - 1 else CHUNK
                    bank = 7 if i % 2 == 0 else 4
                    for g in range(2):
                        last = pe.matmul(ps[HD * g:HD * g + HD, bank, 0:4 * CHUNK],
                                         v_win[0:keys, i, HD * g:HD * g + HD],
                                         prob_t[0:keys, i % 2, 2 * P * g:2 * P * (g + 1)],
                                         start=True, stop=True)
                    last.then_inc(oa_done, 1)

            for n in (V_B0, GATE_B0):
                for q in range(4):
                    chunk(n, q)

            def turn(p, k, groups):
                i = 8 * p + k
                for g in groups:
                    pe.wait_ge(w_ready, 2 * (i + 1))
                    bank = t_bank(T_B + T_PAIR * p + 2 + T_GROUPS * k + g)
                    for b_ in range(4 * g, min(4 * g + 4, SB + 1)):
                        at = P * (b_ % 4)
                        last = pe.transpose(bank[:, at:at + P], beta[:, i % 3, P * b_:P * (b_ + 1)], ident[:])
                    last.then_inc(tp_done, 1)

            def scores(p, k):
                h, tb, n1, tb2, n2 = step(k)
                i = 8 * p + k
                if i > 0:
                    pe.wait_ge(z_free, i)
                for z, t, width in ((z_big, tb, n1), (z_small, tb2, n2)):
                    for at in range(0, width, HALF):
                        m = min(HALF, width - at)
                        for part in range(2):
                            last = pe.matmul(z[:, at:at + m], qs[:, h, P * t:P * (t + 1)],
                                             ks[:, part, h, P * t + at:P * t + at + m],
                                             start=part == 0, stop=part == 1)
                last.then_inc(z_done, 1)

            def values(p, k):
                h, tb, n1, tb2, n2 = step(k)
                i = 8 * p + k
                if i >= 2:
                    pe.wait_ge(o_free, i - 1)
                nb1 = n1 // P
                for b_ in range(SB + 1):
                    if b_ % 4 == 0:
                        pe.wait_ge(tp_free, T_B + T_PAIR * p + 2 + T_GROUPS * k + b_ // 4 + 1)
                    small_b = b_ >= nb1
                    kb = tb2 + b_ - nb1 if small_b else tb + b_
                    last = pe.matmul(ps[HD * h:HD * h + HD, 7, P * small_b:P * small_b + P],
                                     v_n[:, kb, HD * h:HD * h + HD],
                                     w_t[:, b_ // 4, P * (b_ % 4):P * (b_ % 4) + P],
                                     start=b_ in (0, nb1), stop=b_ in (nb1 - 1, SB))
                last.then_inc(o_done, 1)

            for p in range(PAIRS):
                n = LOOP_B + 4 * p
                last_pair = p == PAIRS - 1
                if p > 0:
                    turn(p - 1, 6, (0, 1))
                chunk(n, 0)
                if p > 0:
                    turn(p - 1, 6, (2,))
                chunk(n, 1)
                if p > 0:
                    values(p - 1, 6)
                    turn(p - 1, 7, (0, 1))
                chunk(n, 2)
                if p > 0:
                    turn(p - 1, 7, (2,))
                chunk(n, 3)
                if p > 0:
                    values(p - 1, 7)
                for h in range(2):
                    pe.wait_ge(bank_free[h], V_B0 + 4 * p + 1)
                for g in range(2):
                    bank = t_bank(T_B + T_PAIR * p + g)
                    for b_ in range(4 * g, 4 * g + 4):
                        last = pe.transpose(bank[:, P * (b_ % 4):P * (b_ % 4) + P], v_t[:, P * b_:P * (b_ + 1)],
                                            ident[:])
                    last.then_inc(tp_done, 1)
                for q in range(4):
                    chunk(n + 1, q)
                for k in range(8):
                    if k >= 2:
                        turn(p, k - 2, (0, 1))
                    if not last_pair:
                        chunk(n + 2 + k // 4, k % 4)
                    if k == 0:
                        pe.wait_ge(k_dup, 64 * (p + 2))
                        for h in range(2):
                            pe.wait_ge(bank_free[h], n + 2)
                    scores(p, k)
                    if k >= 2:
                        turn(p, k - 2, (2,))
                        values(p, k - 2)
            for k in (6, 7):
                turn(PAIRS - 1, k, (0, 1, 2))
                values(PAIRS - 1, k)

            for j in range(KT):
                n = LOOP_U + 3 * j
                for q in range(4):
                    chunk(n, q, USE_U + 2 * j)
                pe.wait_ge(lo_done, n + 2)
                if j > 0:
                    pe.wait_ge(yb_mul, 2 * j)
                s = (n + 1) % 2
                for ab in range(2):
                    for h in range(2):
                        for k in range(4):
                            kk = 4 * ab + k
                            if j == 0:
                                pe.wait_ge(ol_done, kk + 1)
                            wk = slice(P * kk, P * (kk + 1))
                            xs = slice(HALF * h, HALF * (h + 1))
                            last = mma3(pe, ps[:, 2 + 2 * ab + h, :], w_hi[:, s, wk], w_lo[:, s, wk],
                                        r_hi[:, kk, xs], r_lo[:, kk, xs], k == 0, k == 3)
                last.then_inc(up_done, 1)
                for q in range(4):
                    chunk(n + 2, q, USE_U + 2 * j + 1)

            pe.wait_ge(yb_mul, 2 * KT)
            for k in range(KT):
                pe.wait_ge(ml_done, k + 1)
                pe.wait_ge(wo_lo, k + 1)
                for s in range(4):
                    for h in range(2):
                        xs, ws = slice(P * s, P * (s + 1)), slice(HALF * h, HALF * (h + 1))
                        last = mma3(pe, ps[:, 2 * s + h, :], x_hi[:, k, xs], x_lo[:, k, xs],
                                    r_hi[:, k, ws], r_lo[:, k, ws], k == 0, k == KT - 1)
                    if k == KT - 1:
                        last.then_inc(r_psum, 1)
            for s in range(4, SB):
                pe.wait_ge(r_set, 2 * (s - 3))
                for h in range(2):
                    for k in range(KT):
                        xs, ws = slice(P * s, P * (s + 1)), slice(HALF * h, HALF * (h + 1))
                        last = mma3(pe, ps[:, 2 * (s % 4) + h, :], x_hi[:, k, xs], x_lo[:, k, xs],
                                    r_hi[:, k, ws], r_lo[:, k, ws], k == 0, k == KT - 1)
                last.then_inc(r_psum, 1)


def columns():
    at = np.cumsum([0, 512, 128, 128, 512, 512, 512, 512, 512, D, D])
    q_a, k_a, v_a, gate_a, q_b, k_b, v_b, gate_b, mg_a, mg_b = at[:-1]
    tile = np.arange(P)

    def heads(base, i):
        return np.concatenate([base + HD * (GROUP * g + i) + np.arange(HD) for g in range(2)])

    order = {K_A: k_a + tile, V_A: v_a + tile}
    for i in range(4):
        order[Q_A + i] = heads(q_a, i)
        order[GATE_A + i] = heads(gate_a, i)
    for p in range(PAIRS):
        order[V_B0 if p == 0 else LOOP_B + 4 * p - 2] = v_b + P * p + tile
        order[GATE_B0 if p == 0 else LOOP_B + 4 * p - 1] = gate_b + P * p + tile
        order[LOOP_B + 4 * p] = k_b + P * p + tile
        order[LOOP_B + 4 * p + 1] = q_b + P * p + tile
    for j in range(KT):
        order[LOOP_U + 3 * j] = mg_a + P * j + tile
        order[LOOP_U + 3 * j + 2] = mg_b + P * j + tile
    return order


def kernel(x, w_in, b_in, sinks, w_up_a, w_up_b, w_out, ln_g, ln_b):
    import concourse.bacc as bacc
    from concourse.bass_utils import run_bass_kernel_spmd

    x, w_in, b_in, sinks, w_up_a, w_up_b, w_out, ln_g, ln_b = (
        np.asarray(t)[0] for t in (x, w_in, b_in, sinks, w_up_a, w_up_b, w_out, ln_g, ln_b))
    backwards = x[::-1]
    w = np.empty((N_TILES, P, D), x.dtype)
    bias = np.zeros((P, LOOP_U + 3 * KT), x.dtype)
    for n, cols in columns().items():
        w[n] = w_in[:, cols].reshape(KT, P, P).transpose(1, 0, 2).reshape(P, D)
        bias[:, n] = b_in[cols]
    up_rows = np.concatenate([HD * (GROUP * g + i) + np.arange(HD) for i in range(4) for g in range(2)])
    up = np.concatenate([w_up_a[up_rows], w_up_b])
    for j in range(KT):
        w[LOOP_U + 3 * j + 1] = up[:, P * j:P * (j + 1)].reshape(KT, P, P).transpose(1, 0, 2).reshape(P, D)
        w[W_OUT + j] = w_out[P * j:P * (j + 1)]
    sink_rows = np.repeat(sinks.reshape(2, 2, 2).transpose(2, 0, 1).reshape(2, GROUP), CHUNK, axis=0)
    half = HD // 2
    freq = np.float32(10000.0) ** (-np.arange(half, dtype=np.float32) / np.float32(half))
    angle = (freq[:, None] * np.arange(SEQ, dtype=np.float32)[None, ::-1]).astype(np.float64)
    cos = np.tile(np.cos(angle), (4, 1)).astype(np.float32)
    sin = np.tile(np.concatenate([-np.sin(angle), np.sin(angle)]), (2, 1)).astype(np.float32)
    arrays = {
        "xt": np.ascontiguousarray(backwards.T).reshape(KT, P, SEQ),
        "xn": np.ascontiguousarray(backwards).reshape(SB, P, D),
        "w": w, "bias": bias, "cos": cos, "sin": sin, "sinks": np.ascontiguousarray(sink_rows),
        "ln_g": np.ascontiguousarray(np.broadcast_to(ln_g, (P, D))),
        "ln_b": np.ascontiguousarray(np.broadcast_to(ln_b, (P, D))),
    }
    nc = bacc.Bacc("TRN2", target_bir_lowering=False, num_devices=1)
    args = [nc.dram_tensor(f"in_{k}", a.shape, mybir.dt.from_np(a.dtype), kind="ExternalInput").ap()
            for k, a in arrays.items()]
    out = nc.dram_tensor("out_0", (SB, P, D), F32, kind="ExternalOutput").ap()
    build(nc, *args, out)
    r = run_bass_kernel_spmd(nc, [{f"in_{k}": a for k, a in arrays.items()}], core_ids=[0])
    return r.results[0]["out_0"].reshape(SEQ, D)[::-1].reshape(1, SEQ, D)
```

```python
from contextlib import ExitStack

import numpy as np

import concourse.bass as bass
from concourse import mybir

F32 = mybir.dt.float32
F32R = mybir.dt.float32r
ACT = mybir.ActivationFunctionType
ALU = mybir.AluOpType
AX_X = mybir.AxisListType.X

P = 128
SEQ = 1024
D = 1024
HD = 64
KT = D // P
SB = SEQ // P
HALF = 512
CHUNK = 64
NCHUNK = SEQ // CHUNK
GROUP = 4
PAIRS = 4
SCALE = HD ** -0.5
ALPHA = 2.0 ** 0.25
LN_EPS = 1e-5

K_A, V_A, Q_A, GATE_A = 0, 1, 2, 6
V_B0, GATE_B0, LOOP_B = 10, 11, 12
MG_0 = LOOP_B + 4 * PAIRS - 2
LOOP_U = MG_0 + 2
W_OUT = MG_0 + 3 * KT
N_TILES = W_OUT + KT
USE_U = MG_0
STEP_COLS = SEQ + P
T_GROUPS = 3
T_PAIR = 2 + 8 * T_GROUPS


def up_tile(j):
    return LOOP_U + 3 * j + 1 if j < KT - 1 else W_OUT - 1


def merge_tile(j, ab):
    return MG_0 + ab if j == 0 else LOOP_U + 3 * (j - 1) + 2 * ab


def out_bank(s, h):
    return (0, 6, 2, 4)[s % 4] + h


def mma3(pe, out, w_hi, w_lo, x_hi, x_lo, first, last):
    pe.matmul(out, w_hi, x_hi, start=first, stop=False)
    pe.matmul(out, w_hi, x_lo, start=False, stop=False)
    return pe.matmul(out, w_lo, x_hi, start=False, stop=last)


def build(nc, xt, xn, w, bias, cos, sin, sinks, ln_g, ln_b, out):
    with ExitStack() as ctx:
        def sb(name, shape, dt=F32, where=ctx):
            return where.enter_context(nc.sbuf_tensor(name, shape, dt))

        def sem(name):
            return ctx.enter_context(nc.semaphore(name))

        x_hi = sb("x_hi", [P, KT, SEQ], F32R)
        x_lo = sb("x_lo", [P, KT, SEQ], F32R)
        raw = sb("raw", [P, 2, D])
        w_hi = sb("w_hi", [P, 2, D], F32R)
        w_lo = sb("w_lo", [P, 2, D], F32R)
        o_t = sb("o_t", [P, KT, SEQ])
        v_t = sb("v_t", [P, SEQ])
        ident = sb("ident", [P, P])
        later = sb("later", [P, P])
        bias_c = sb("bias_c", [P, W_OUT])
        sink_c = sb("sink_c", [P, GROUP])
        nsink_c = sb("nsink_c", [P, GROUP])
        small = sb("small", [P, 8, 8])
        eps_c = sb("eps_c", [P, 1])
        sig_m = sb("sig_m", [P, 6, HALF])
        sig_g = sig_m[:, 2, :]
        o_part = sig_m[:, 3, :]
        cos_t, sin_t = o_t[:, 0, :], o_t[:, 1, :]
        ps = ctx.enter_context(nc.psum_tensor("ps", [P, 8, HALF], F32))

        x_in = [sem(f"x_in{k}") for k in range(2 * KT)]
        raw_in = [sem(f"raw_in{i}") for i in range(2)]
        const_in = sem("const_in")
        rope_in = sem("rope_in")
        ln_in = sem("ln_in")
        xn_in = [sem(f"xn_in{i}") for i in range(2)]
        k_dup = sem("k_dup")
        out_done = [sem(f"out_done{i}") for i in range(2)]
        masks = sem("masks")
        eps_set = sem("eps_set")
        ones_set, sink_set, stick_ones = sem("ones_set"), sem("sink_set"), sem("stick_ones")
        x_hi_done, x_lo_done = sem("x_hi_done"), sem("x_lo_done")
        hi_done, lo_done = sem("hi_done"), sem("lo_done")
        half_done = sem("half_done")
        bank_free = [sem("bank_free0"), sem("bank_free1")]
        swapped = sem("swapped")
        dve_rope = sem("dve_rope")
        rope_done = sem("rope_done")
        split_hi = sem("split_hi")
        k_split = sem("k_split")
        q_split = sem("q_split")
        gate_sig = sem("gate_sig")
        tp_done, tp_free = sem("tp_done"), sem("tp_free")
        tb_done, tb_hi, tb_free = sem("tb_done"), sem("tb_hi"), sem("tb_free")
        o_copied, o_summed, o_set = sem("o_copied"), sem("o_summed"), sem("o_set")
        za_done, za_max, za_bias, za_exp, za_sum, za_p = (
            sem("za_done"), sem("za_max"), sem("za_bias"), sem("za_exp"), sem("za_sum"), sem("za_p"))
        oa_done, oa_free = sem("oa_done"), sem("oa_free")
        ga_sig, ga_mul, ga_set = sem("ga_sig"), sem("ga_mul"), sem("ga_set")
        z_done, z_free = sem("z_done"), sem("z_free")
        masked, kept, scanned, w_ready = sem("masked"), sem("kept"), sem("scanned"), sem("w_ready")
        o_done, o_free = sem("o_done"), sem("o_free")
        oh_done, ol_done = sem("oh_done"), sem("ol_done")
        up_done, mg_sig, ya_mul, yb_mul, m_set = (
            sem("up_done"), sem("mg_sig"), sem("ya_mul"), sem("yb_mul"), sem("m_set"))
        mh_done, ml_done, wo_hi, wo_lo = sem("mh_done"), sem("ml_done"), sem("wo_hi"), sem("wo_lo")
        r_psum, r_set, ln_chain, ln_var, ln_std, ln_nb, ln_norm, ln_out = (
            sem("r_psum"), sem("r_set"), sem("ln_chain"), sem("ln_var"), sem("ln_std"),
            sem("ln_nb"), sem("ln_norm"), sem("ln_out"))

        with ExitStack() as a:
            qa = sb("qa", [P, 2, NCHUNK, GROUP, CHUNK], F32R, a)
            ka = sb("ka", [P, 2, 2, SEQ], F32R, a)
            v_win = sb("v_win", [P, NCHUNK, P], F32, a)
            prob = sb("prob", [P, 3, HALF], F32, a)
            prob_t = sb("prob_t", [P, 2, HALF], F32, a)
        with ExitStack() as b:
            qs = sb("qs", [P, 2, SEQ], F32R, b)
            ks = sb("ks", [P, 2, 2, SEQ], F32R, b)
            v_n = sb("v_n", [P, SB, 2, 2, HD], F32R, b)
            beta = sb("beta", [P, 2, STEP_COLS], F32, b)
            keep = sb("keep", [P, 2, STEP_COLS], F32, b)
            stick = sb("stick", [P, SEQ + 1], F32, b)
            w_t = sb("w_t", [P, SB + 1, 2, P], F32R, b)
        with ExitStack() as u:
            r_hi = sb("r_hi", [P, KT, SEQ], F32R, u)
            r_lo = sb("r_lo", [P, KT, SEQ], F32R, u)
        g_bc = sig_m[:, 0:2, :].rearrange("p a b -> p (a b)")
        b_bc = sig_m[:, 2:4, :].rearrange("p a b -> p (a b)")

        block = ctx.enter_context(nc.Block())
        z_big = ps[:, 2:4, :].rearrange("p a b -> p (a b)")
        z_small = ps[:, 4, :]

        def step(k):
            h, j = k % 2, k // 2
            return h, j, SEQ - P * j, SB - 1 - j, P * (j + 1)

        @block.sync
        def _(sp):
            def load_w(n):
                if n >= 2:
                    if n - 2 < W_OUT:
                        sp.wait_ge(lo_done, n - 1)
                    else:
                        sp.wait_ge(wo_lo, n - 1 - W_OUT)
                sp.dma_start(raw[:, n % 2, :], w[n]).then_inc(raw_in[n % 2], 16)

            def duplicate_keys(keys):
                for part in range(2):
                    for g in range(2):
                        have, want = slice(HD * g, HD * g + HD), slice(HD - HD * g, P - HD * g)
                        sp.dma_start(keys[want, part, g, :].bitcast(F32),
                                     keys[have, part, g, :].bitcast(F32)).then_inc(k_dup, 16)

            load_w(0)
            for h in range(2):
                cols = slice(HALF * h, HALF * (h + 1))
                for k in range(KT):
                    sp.dma_start(o_t[:, k, cols], xt[k][:, cols]).then_inc(x_in[KT * h + k], 16)
                if h == 0:
                    for dst, src in ((bias_c, bias), (sink_c, sinks)):
                        sp.dma_start(dst[:], src).then_inc(const_in, 16)
                    load_w(1)
            sp.wait_ge(x_lo_done, KT + 2)
            sp.dma_start(cos_t, cos).then_inc(rope_in, 16)
            sp.dma_start(sin_t, sin).then_inc(rope_in, 16)
            load_w(2)
            load_w(3)
            for n in range(4, LOOP_B + 4):
                if n == 5:
                    sp.wait_ge(k_split, 4)
                    duplicate_keys(ka)
                load_w(n)
            for p in range(PAIRS):
                sp.wait_ge(bank_free[0], LOOP_B + 4 * p + 1)
                sp.wait_ge(bank_free[1], LOOP_B + 4 * p + 1)
                duplicate_keys(ks)
                if p < PAIRS - 1:
                    for i in range(4):
                        load_w(LOOP_B + 4 * (p + 1) + i)
            for n in range(LOOP_B + 4 * PAIRS, N_TILES):
                load_w(n)
            sp.wait_ge(m_set, 2 * KT)
            sp.dma_start(g_bc, ln_g).then_inc(ln_in, 16)
            sp.dma_start(b_bc, ln_b).then_inc(ln_in, 16)
            sp.wait_ge(wo_lo, KT)

            def store_rows(s):
                for h in range(2):
                    cols = slice(HALF * h, HALF * (h + 1))
                    sp.wait_ge(ln_out, 2 * s + h + 1)
                    sp.dma_start(out[s][:, cols], o_t[:, 2 + s % 2, cols]).then_inc(out_done[s % 2], 16)

            for s in range(SB):
                if s >= 2:
                    sp.wait_ge(r_set, 2 * (s - 1))
                sp.dma_start(raw[:, s % 2, :], xn[s]).then_inc(xn_in[s % 2], 16)
                if s >= 1:
                    store_rows(s - 1)
            store_rows(SB - 1)
            sp.wait_ge(out_done[0], 32 * (SB // 2))
            sp.wait_ge(out_done[1], 32 * (SB // 2))

        @block.gpsimd
        def _(pool):
            pool.memset(ident[:], 0.0).then_inc(ones_set, 1)
            pool.memset(later[:], 1.0).then_inc(ones_set, 1)
            pool.wait_ge(ones_set, 2)
            pool.affine_select(out=ident[:], in_=ident[:], compare_op=ALU.not_equal, fill=1.0, base=0,
                               pattern=[[-1, P]], channel_multiplier=1).then_inc(masks, 1)
            pool.affine_select(out=later[:], in_=later[:], compare_op=ALU.is_gt, fill=0.0, base=0,
                               pattern=[[1, P]], channel_multiplier=-1).then_inc(masks, 1)
            def low_weights(n):
                pool.wait_ge(hi_done, n + 1)
                pool.tensor_tensor(w_lo[:, n % 2, :], raw[:, n % 2, :], w_hi[:, n % 2, :].bitcast(F32),
                                   ALU.subtract).then_inc(lo_done, 1)

            def keeps(p, k):
                h, tb, n1, tb2, n2 = step(k)
                i = 8 * p + k
                bt = beta[:, i % 2, :]
                pool.wait_ge(z_free, i + 1)
                for at in (0, n1):
                    pool.tensor_tensor(bt[:, at:at + P], bt[:, at:at + P], later[:], ALU.mult).then_inc(masked, 1)
                pool.wait_ge(masked, 2 * (i + 1))
                if i >= 2:
                    pool.wait_ge(w_ready, 2 * (i - 1))
                pool.tensor_scalar(keep[:, i % 2, :], bt, -1.0, 1.0, ALU.mult, ALU.add).then_inc(kept, 1)

            for n in range(LOOP_B + 2):
                low_weights(n)
            pool.wait_ge(masks, 2)
            for p in range(PAIRS):
                n = LOOP_B + 4 * p
                low_weights(n + 2)
                low_weights(n + 3)
                for k in range(8):
                    keeps(p, k)
                    if k % 4 == 3:
                        low_weights(n + 4 + k // 4)
            for n in range(LOOP_B + 4 * PAIRS + 2, W_OUT):
                low_weights(n)

        @block.scalar
        def _(act):
            def tile_used(n):
                j, i = divmod(n - LOOP_U, 3)
                if n < LOOP_U:
                    act.wait_ge(half_done, 2 * n + 2)
                elif i == 1:
                    act.wait_ge(up_done, j + 1)
                else:
                    act.wait_ge(half_done, 2 * (USE_U + 2 * (j + 1) + i // 2) + 2)

            def weight_hi(n):
                if n >= W_OUT:
                    return
                act.wait_ge(raw_in[n % 2], 16 * (n // 2 + 1))
                if n >= 2:
                    tile_used(n - 2)
                act.activation(w_hi[:, n % 2, :], raw[:, n % 2, :], ACT.Copy).then_inc(hi_done, 1)

            def half(h):
                return slice(HALF * h, HALF * (h + 1))

            def b_of(n, lo=0, hi=P):
                return bias_c[lo:hi, n:n + 1]

            def rope_index(n, h):
                return 2 * (n if n == K_A else n - 1) + h

            def rope_swap(n, h):
                i = rope_index(n, h)
                act.wait_ge(half_done, 2 * n + h + 1)
                if i >= 2:
                    act.wait_ge(rope_done, i - 1)
                for q in range(4):
                    o = 32 * (q ^ 1)
                    act.activation(sig_m[o:o + 32, i % 2, :], ps[32 * q:32 * q + 32, h, :], ACT.Identity,
                                   bias=b_of(n, 32 * q, 32 * q + 32)).then_inc(swapped, 1)

            def rope_hi(n, h):
                i = rope_index(n, h)
                act.wait_ge(rope_done, i + 1)
                for g in range(2):
                    r = slice(HD * g, HD * g + HD)
                    rot = sig_m[r, 2 + i % 2, :]
                    if n == K_A:
                        dst, src = ka[r, 0, g, half(h)], rot
                    else:
                        dst = qa[r, g, 8 * h:8 * h + 8, n - Q_A, :]
                        src = rot.rearrange("p (c t) -> p c t", t=CHUNK)
                    act.activation(dst, src, ACT.Copy).then_inc(split_hi, 1)

            def head_hi(n, h, dst):
                act.wait_ge(half_done, 2 * n + h + 1)
                for g in range(2):
                    r = slice(HD * g, HD * g + HD)
                    act.activation(dst[r, g, half(h)], ps[r, h, :], ACT.Identity,
                                   bias=b_of(n, HD * g, HD * g + HD)).then_inc(split_hi, 1)

            def value_half(n, h):
                act.wait_ge(half_done, 2 * n + h + 1)
                act.activation(v_t[:, half(h)], ps[:, h, :], ACT.Identity,
                               bias=b_of(n)).then_inc(bank_free[h], 1)

            def gate_b_half(n, h):
                act.wait_ge(half_done, 2 * n + h + 1)
                if h == 1:
                    act.wait_ge(bank_free[0], n + 1)
                elif n > GATE_B0:
                    act.wait_ge(bank_free[1], n - 3)
                act.activation(sig_g[:], ps[:, h, :], ACT.Sigmoid, bias=b_of(n)).then_inc(gate_sig, 1)

            weight_hi(0)
            for h in range(2):
                for k in range(KT):
                    act.wait_ge(x_in[KT * h + k], 16)
                    act.activation(x_hi[:, k, half(h)], o_t[:, k, half(h)], ACT.Copy).then_inc(x_hi_done, 1)
                if h == 0:
                    weight_hi(1)
            act.wait_ge(const_in, 32)
            def window_group(i):
                act.wait_ge(tp_done, i + 1)
                src = ps[:, 5 + i % 2, :]
                full = 4 if i < 3 else 3
                ins = act.activation(v_win[:, 4 * i:4 * i + full, :].rearrange("p a b -> p (a b)"),
                                     src[:, 0:P * full], ACT.Copy)
                if i == 3:
                    ins = act.activation(v_win[0:CHUNK, NCHUNK - 1, :],
                                         src[0:CHUNK, P * 3:P * 4], ACT.Copy)
                ins.then_inc(tp_free, 1)

            before = None
            for n in range(0, GATE_A):
                if n > Q_A:
                    window_group(n - Q_A - 1)
                for h in range(2):
                    if n == V_A:
                        value_half(n, h)
                    else:
                        rope_swap(n, h)
                    if before:
                        rope_hi(*before)
                    before = None if n == V_A else (n, h)
                weight_hi(n + 2)
            rope_hi(*before)
            window_group(3)
            for c in range(NCHUNK + 2):
                if c >= 2:
                    i = c - 2
                    rows = P if i < NCHUNK - 1 else CHUNK
                    act.wait_ge(tp_done, 4 + i + 1)
                    if i >= 2:
                        act.wait_ge(oa_done, i - 1)
                    act.activation(prob_t[0:rows, i % 2, :], ps[0:rows, 5 + i % 2, :],
                                   ACT.Copy).then_inc(tp_free, 1)
                if c < NCHUNK:
                    if c % 2 == 0:
                        n, h = GATE_A + c // 4, (c % 4) // 2
                        act.wait_ge(half_done, 2 * n + h + 1)
                        act.activation(o_t[:, 4 + c // 4, half(h)], ps[:, h, :], ACT.Identity,
                                       bias=b_of(n)).then_inc(bank_free[h], 1)
                    if c % 4 == 2:
                        weight_hi(GATE_A + c // 4 + 2)
                    keys = P if c < NCHUNK - 1 else CHUNK
                    act.wait_ge(za_bias, 2 * (c + 1))
                    sm = small[:, c % 2 * 3:c % 2 * 3 + 3, :]
                    act.activation(sm[:, 2, 0:4], sm[:, 1, 0:4], ACT.Exp).then_inc(za_exp, 1)
                    for cb in range(4):
                        act.activation(prob[:, c % 3, P * cb:P * cb + keys],
                                       ps[:, 2 + c % 2, P * cb:P * cb + keys], ACT.Exp,
                                       bias=sm[:, 0, cb:cb + 1], scale=SCALE,
                                       accum_out=sm[:, 2, 4 + cb:5 + cb]).then_inc(za_exp, 1)
            value_half(V_B0, 0)
            value_half(V_B0, 1)
            weight_hi(V_B0 + 2)
            act.wait_ge(oa_free, NCHUNK)
            for i in range(4):
                if i >= 2:
                    act.wait_ge(ga_set, i - 1)
                act.activation(beta[:, i % 2, 0:SEQ], o_t[:, 4 + i, :], ACT.Sigmoid).then_inc(ga_sig, 1)
            for h in range(2):
                gate_b_half(GATE_B0, h)
            weight_hi(GATE_B0 + 2)

            def turned_hi(p, k):
                for g in range(T_GROUPS):
                    i = T_PAIR * p + 2 + T_GROUPS * k + g
                    nb = 4 if g < 2 else 1
                    act.wait_ge(tb_done, i + 1)
                    act.activation(w_t[:, 4 * g:4 * g + nb, 0, :],
                                   ps[:, 5 + i % 2, 0:P * nb].rearrange("p (a t) -> p a t", t=P),
                                   ACT.Copy).then_inc(tb_hi, 1)

            def values_hi(p):
                for g in range(2):
                    i = T_PAIR * p + g
                    act.wait_ge(tb_done, i + 1)
                    act.activation(v_n[:, 4 * g:4 * g + 4, :, 0, :],
                                   ps[:, 5 + i % 2, :].rearrange("p (a h d) -> p a h d", h=2, d=HD),
                                   ACT.Copy).then_inc(tb_hi, 1)

            def betas(p, k):
                h, tb, n1, tb2, n2 = step(k)
                i = 8 * p + k
                act.wait_ge(z_done, i + 1)
                dst = beta[:, i % 2, :]
                if i == 0:
                    act.wait_ge(ga_set, 4)
                act.activation(dst[:, 0:n1], z_big[:, 0:n1], ACT.Sigmoid, scale=SCALE)
                act.activation(dst[:, n1:n1 + n2], z_small[:, 0:n2], ACT.Sigmoid,
                               scale=SCALE).then_inc(z_free, 1)

            def copy_out(p, k):
                h = k % 2
                i = 8 * p + k
                act.wait_ge(o_done, i + 1)
                if i >= 1:
                    act.wait_ge(o_set, 2 * i)
                act.activation(o_part[HD * h:HD * h + HD, :], ps[HD - HD * h:P - HD * h, 7, :],
                               ACT.Copy).then_inc(o_copied, 1)

            def merge_gate(j, ab, h):
                act.wait_ge(half_done, 2 * (USE_U + 2 * j + ab) + h + 1)
                if ab == 0 and j >= 2:
                    act.wait_ge(m_set, 2 * (j - 2) + h + 1)
                if ab == 1 and j >= 1:
                    act.wait_ge(m_set, 2 * (j - 1) + h + 1)
                act.activation(sig_m[:, 4 * ab + (2 * (j % 2) if ab == 0 else 0) + h, :], ps[:, h, :],
                               ACT.Sigmoid, bias=b_of(merge_tile(j, ab))).then_inc(mg_sig, 1)

            for p in range(PAIRS):
                n = LOOP_B + 4 * p
                last = p == PAIRS - 1
                if p > 0:
                    turned_hi(p - 1, 6)
                    copy_out(p - 1, 6)
                head_hi(n, 0, ks[:, 0])
                if p > 0:
                    turned_hi(p - 1, 7)
                    copy_out(p - 1, 7)
                head_hi(n, 1, ks[:, 0])
                weight_hi(n + 2)
                values_hi(p)
                head_hi(n + 1, 0, qs)
                head_hi(n + 1, 1, qs)
                weight_hi(n + 3)
                for k in range(8):
                    if k >= 2:
                        turned_hi(p, k - 2)
                    if k % 2 == 1:
                        if last:
                            merge_gate(0, k // 4, (k // 2) % 2)
                        elif k < 4:
                            value_half(n + 2, k // 2)
                        else:
                            gate_b_half(n + 3, (k - 4) // 2)
                    if k % 4 == 3:
                        weight_hi(n + 4 + k // 4)
                    betas(p, k)
                    if k >= 2:
                        copy_out(p, k - 2)
            for k in (6, 7):
                turned_hi(PAIRS - 1, k)
                copy_out(PAIRS - 1, k)
            act.wait_ge(o_set, 16 * PAIRS)
            for k in range(KT):
                act.activation(r_hi[:, k, :], o_t[:, k, :], ACT.Copy).then_inc(oh_done, 1)
            for j in range(1, KT):
                n = LOOP_U + 3 * (j - 1)
                weight_hi(n + 2)
                for h in range(2):
                    merge_gate(j, 0, h)
                weight_hi(n + 3)
                for h in range(2):
                    merge_gate(j, 1, h)
                weight_hi(n + 4)
            def merged_hi(k):
                act.activation(x_hi[:, k, :], o_t[:, k, :], ACT.Copy).then_inc(mh_done, 1)

            def w_out_hi(k):
                n = W_OUT + k
                act.wait_ge(raw_in[n % 2], 16 * (n // 2 + 1))
                act.activation(r_hi[:, k, :], raw[:, n % 2, :], ACT.Copy).then_inc(wo_hi, 1)

            act.wait_ge(m_set, 2 * (KT - 1))
            for k in range(KT - 1):
                merged_hi(k)
            act.wait_ge(up_done, KT)
            for k in range(KT):
                w_out_hi(k)
                if k == 1:
                    act.wait_ge(m_set, 2 * KT)
                    merged_hi(KT - 1)
            for s in range(SB):
                act.wait_ge(ln_var, s + 1)
                st = small[:, s % 2, :]
                act.activation(st[:, 2:3], st[:, 1:2], ACT.Sqrt, bias=eps_c[:, 0:1]).then_inc(ln_std, 1)
                act.wait_ge(ln_nb, s + 1)
                for h in range(2):
                    act.activation(o_t[:, s % 2, half(h)], o_t[:, s % 2, half(h)], ACT.Identity,
                                   bias=st[:, 4:5], scale=st[:, 3:4]).then_inc(ln_norm, 1)

        @block.vector
        def _(dve):
            def half(h):
                return slice(HALF * h, HALF * (h + 1))

            def b_of(n, lo=0, hi=P):
                return bias_c[lo:hi, n:n + 1]

            def rope_index(n, h):
                return 2 * (n if n == K_A else n - 1) + h

            def rotate(n, h):
                i = rope_index(n, h)
                t_swap, t_rot, t_cos = (sig_m[:, 2 * q + i % 2, :] for q in range(3))
                dve.wait_ge(swapped, 4 * (i + 1))
                if i >= 2:
                    dve.wait_ge(rope_done, i - 1)
                dve.scalar_tensor_tensor(out=t_cos, in0=ps[:, h, :], scalar=b_of(n), in1=cos_t[:, half(h)],
                                         op0=ALU.add, op1=ALU.mult).then_inc(bank_free[h], 1)
                dve.tensor_tensor(t_swap, t_swap, sin_t[:, half(h)], ALU.mult).then_inc(dve_rope, 1)
                dve.wait_ge(bank_free[h], n + 1)
                dve.wait_ge(dve_rope, i + 1)
                if i >= 2:
                    dve.wait_ge(split_hi, 2 * (i - 1))
                dve.tensor_tensor(t_rot, t_cos, t_swap, ALU.add).then_inc(rope_done, 1)

            def rope_lo(n, h):
                i = rope_index(n, h)
                dve.wait_ge(rope_done, i + 1)
                for g in range(2):
                    r = slice(HD * g, HD * g + HD)
                    o = slice(HD - HD * g, P - HD * g)
                    rot = sig_m[r, 2 + i % 2, :]
                    dve.wait_ge(split_hi, 2 * i + g + 1)
                    if n == K_A:
                        dve.tensor_tensor(ka[r, 1, g, half(h)], rot, ka[r, 0, g, half(h)].bitcast(F32),
                                          ALU.subtract).then_inc(k_split, 1)
                    else:
                        dve.tensor_tensor(
                            qa[o, g, 8 * h:8 * h + 8, n - Q_A, :], rot.rearrange("p (c t) -> p c t", t=CHUNK),
                            qa[r, g, 8 * h:8 * h + 8, n - Q_A, :].bitcast(F32),
                            ALU.subtract).then_inc(q_split, 1)

            ROPE_HI = 2 * 2 * 5

            def head_lo(p, n, h, dst, is_key):
                i = ROPE_HI + 8 * p + (0 if is_key else 4) + 2 * h
                dve.wait_ge(split_hi, i + 2)
                for g in range(2):
                    r = slice(HD * g, HD * g + HD)
                    o = slice(HD - HD * g, P - HD * g)
                    if is_key:
                        hi_part, to = dst[r, 0, g, half(h)], dst[r, 1, g, half(h)]
                    else:
                        hi_part, to = dst[r, g, half(h)], dst[o, g, half(h)]
                    ins = dve.scalar_tensor_tensor(out=to, in0=ps[r, h, :], scalar=b_of(n, HD * g, HD * g + HD),
                                                   in1=hi_part.bitcast(F32), op0=ALU.add, op1=ALU.subtract)
                ins.then_inc(bank_free[h], 1)

            def gate_b_half(n, h):
                p = (n - GATE_B0) // 4
                dve.wait_ge(gate_sig, 2 * p + h + 1)
                dve.scalar_tensor_tensor(out=o_t[:, 4 + p, half(h)], in0=ps[:, h, :], scalar=b_of(n),
                                         in1=sig_g[:], op0=ALU.add, op1=ALU.mult).then_inc(bank_free[h], 1)

            dve.memset(eps_c[:], LN_EPS).then_inc(eps_set, 1)
            for h in range(2):
                for k in range(KT):
                    dve.wait_ge(x_hi_done, KT * h + k + 1)
                    dve.tensor_tensor(x_lo[:, k, half(h)], o_t[:, k, half(h)], x_hi[:, k, half(h)].bitcast(F32),
                                      ALU.subtract).then_inc(x_lo_done, 1)
            dve.wait_ge(const_in, 32)
            dve.tensor_scalar(nsink_c[:], sink_c[:], -1.0, None, ALU.mult).then_inc(sink_set, 1)
            dve.wait_ge(rope_in, 32)
            before = None
            for n in range(0, GATE_A):
                if n != V_A:
                    for h in range(2):
                        rotate(n, h)
                        if before:
                            rope_lo(*before)
                        before = (n, h)
            rope_lo(*before)

            def prob_norm(c):
                keys = P if c < NCHUNK - 1 else CHUNK
                sm = small[:, c % 2 * 3:c % 2 * 3 + 3, :]
                dve.wait_ge(za_exp, 5 * (c + 1))
                dve.tensor_tensor(sm[:, 2, 0:4], sm[:, 2, 0:4], sm[:, 2, 4:8], ALU.add).then_inc(za_sum, 1)
                dve.wait_ge(za_sum, 2 * c + 1)
                dve.reciprocal(sm[:, 2, 0:4], sm[:, 2, 0:4]).then_inc(za_sum, 1)
                dve.wait_ge(za_sum, 2 * c + 2)
                pr = prob[:, c % 3, :].rearrange("p (a k) -> p a k", k=P)[:, :, 0:keys]
                dve.tensor_tensor(pr, pr, sm[:, 2, 0:4].unsqueeze(2).to_broadcast([P, 4, keys]),
                                  ALU.mult).then_inc(za_p, 1)

            dve.wait_ge(sink_set, 1)
            for c in range(NCHUNK + 3):
                if 1 <= c <= NCHUNK:
                    prob_norm(c - 1)
                if c < NCHUNK:
                    keys = P if c < NCHUNK - 1 else CHUNK
                    sm = small[:, c % 2 * 3:c % 2 * 3 + 3, :]
                    dve.wait_ge(za_done, c + 1)
                    z = ps[:, 2 + c % 2, :].rearrange("p (a k) -> p a k", k=P)[:, :, 0:keys]
                    dve.tensor_reduce(sm[:, 0, 4:8], z, AX_X, ALU.max).then_inc(za_max, 1)
                    dve.wait_ge(za_max, c + 1)
                    dve.scalar_tensor_tensor(out=sm[:, 0, 0:4], in0=sm[:, 0, 4:8], scalar=-SCALE,
                                             in1=nsink_c[:], op0=ALU.mult, op1=ALU.min).then_inc(za_bias, 1)
                    dve.wait_ge(za_bias, 2 * c + 1)
                    dve.tensor_tensor(sm[:, 1, 0:4], sm[:, 0, 0:4], sink_c[:], ALU.add).then_inc(za_bias, 1)
                if c >= 3:
                    i = c - 3
                    dve.wait_ge(oa_done, i + 1)
                    bank = 7 if i % 2 == 0 else 4
                    dve.tensor_copy(o_t[:, 0:4, CHUNK * i:CHUNK * (i + 1)],
                                    ps[:, bank, 0:4 * CHUNK].rearrange("p (a t) -> p a t", t=CHUNK)
                                    ).then_inc(oa_free, 1)
            for i in range(4):
                dve.wait_ge(ga_sig, i + 1)
                sg = beta[:, i % 2, 0:SEQ]
                dve.tensor_tensor(sg, sg, o_t[:, 4 + i, :], ALU.mult).then_inc(ga_mul, 1)
                dve.wait_ge(ga_mul, i + 1)
                if i == 0:
                    dve.wait_ge(oa_free, NCHUNK)
                dve.tensor_tensor(o_t[:, i, :], o_t[:, i, :], sg, ALU.mult).then_inc(ga_set, 1)
            dve.memset(stick[:, 0:1], 1.0).then_inc(stick_ones, 1)
            for h in range(2):
                gate_b_half(GATE_B0, h)

            def break_sticks(p, k):
                h, tb, n1, tb2, n2 = step(k)
                i = 8 * p + k
                bt, kp = beta[:, i % 2, :], keep[:, i % 2, :]
                dve.wait_ge(kept, i + 1)
                for q, (at, m) in enumerate(((0, n1), (n1, n2))):
                    if i + q > 0:
                        dve.wait_ge(w_ready, 2 * i + q)
                    dve.tensor_tensor_scan(stick[:, 1:m + 1], kp[:, at:at + m], kp[:, at:at + m], 1.0,
                                           ALU.mult, ALU.bypass).then_inc(scanned, 1)
                    dve.wait_ge(scanned, 2 * i + q + 1)
                    dve.tensor_tensor(bt[:, at:at + m], bt[:, at:at + m], stick[:, 0:m],
                                      ALU.mult).then_inc(w_ready, 1)

            def turned_lo(p, k, groups):
                for g in groups:
                    i = T_PAIR * p + 2 + T_GROUPS * k + g
                    nb = 4 if g < 2 else 1
                    dve.wait_ge(tb_hi, i + 1)
                    dve.tensor_tensor(w_t[:, 4 * g:4 * g + nb, 1, :],
                                      ps[:, 5 + i % 2, 0:P * nb].rearrange("p (a t) -> p a t", t=P),
                                      w_t[:, 4 * g:4 * g + nb, 0, :].bitcast(F32),
                                      ALU.subtract).then_inc(tb_free, 1)

            def values_lo(p):
                for g in range(2):
                    i = T_PAIR * p + g
                    dve.wait_ge(tb_hi, i + 1)
                    dve.tensor_tensor(v_n[:, 4 * g:4 * g + 4, :, 1, :],
                                      ps[:, 5 + i % 2, :].rearrange("p (a h d) -> p a h d", h=2, d=HD),
                                      v_n[:, 4 * g:4 * g + 4, :, 0, :].bitcast(F32),
                                      ALU.subtract).then_inc(tb_free, 1)

            def store_out(p, k):
                h, tb, n1, tb2, n2 = step(k)
                i = 8 * p + k
                r = slice(HD * h, HD * h + HD)
                dve.wait_ge(o_copied, i + 1)
                dve.tensor_tensor(o_part[r, :], ps[r, 7, :], o_part[r, :], ALU.add).then_inc(o_free, 1)
                dve.wait_ge(o_free, i + 1)
                both = o_part[r, :].rearrange("p (q s t) -> p q s t", q=2, s=2)
                dve.tensor_tensor(both[:, :, 0, :], both[:, :, 0, :], both[:, :, 1, :],
                                  ALU.add).then_inc(o_summed, 1)
                dve.wait_ge(o_summed, i + 1)
                for q, t in ((0, tb), (1, tb2)):
                    o = o_t[r, 4 + p, P * t:P * (t + 1)]
                    dve.tensor_tensor(o, o, both[:, q, 0, :], ALU.mult).then_inc(o_set, 1)

            dve.wait_ge(stick_ones, 1)
            for p in range(PAIRS):
                n = LOOP_B + 4 * p
                last = p == PAIRS - 1
                if p > 0:
                    turned_lo(p - 1, 6, (0, 1))
                    break_sticks(p - 1, 7)
                    turned_lo(p - 1, 6, (2,))
                    store_out(p - 1, 6)
                head_lo(p, n, 0, ks, True)
                if p > 0:
                    turned_lo(p - 1, 7, (0, 1, 2))
                    store_out(p - 1, 7)
                head_lo(p, n, 1, ks, True)
                values_lo(p)
                head_lo(p, n + 1, 0, qs, False)
                head_lo(p, n + 1, 1, qs, False)
                dve.wait_ge(bank_free[0], GATE_B0 + 4 * p + 1)
                dve.wait_ge(bank_free[1], GATE_B0 + 4 * p + 1)
                for k in range(8):
                    if k >= 2:
                        turned_lo(p, k - 2, (0, 1))
                    if k >= 1:
                        break_sticks(p, k - 1)
                    if k >= 2:
                        turned_lo(p, k - 2, (2,))
                    if not last and k >= 4 and k % 2 == 1:
                        gate_b_half(n + 3, (k - 4) // 2)
                    if k >= 2:
                        store_out(p, k - 2)
            turned_lo(PAIRS - 1, 6, (0, 1))
            break_sticks(PAIRS - 1, 7)
            turned_lo(PAIRS - 1, 6, (2,))
            store_out(PAIRS - 1, 6)
            turned_lo(PAIRS - 1, 7, (0, 1, 2))
            store_out(PAIRS - 1, 7)
            dve.wait_ge(o_set, 16 * PAIRS)
            for k in range(KT):
                dve.wait_ge(oh_done, k + 1)
                dve.tensor_tensor(r_lo[:, k, :], o_t[:, k, :], r_hi[:, k, :].bitcast(F32),
                                  ALU.subtract).then_inc(ol_done, 1)

            def merge(j):
                dve.wait_ge(up_done, j + 1)
                dve.wait_ge(mg_sig, 4 * j + 4)
                for h in range(2):
                    sig_a, sig_b = sig_m[:, 2 * (j % 2) + h, :], sig_m[:, 4 + h, :]
                    dve.tensor_tensor(sig_a, sig_a, ps[:, 2 + h, :], ALU.mult).then_inc(ya_mul, 1)
                    dve.tensor_tensor(sig_b, sig_b, ps[:, 4 + h, :], ALU.mult).then_inc(yb_mul, 1)
                    dve.wait_ge(ya_mul, 2 * j + h + 1)
                    dve.wait_ge(yb_mul, 2 * j + h + 1)
                    dve.tensor_tensor(o_t[:, j, half(h)], sig_a, sig_b, ALU.add).then_inc(m_set, 1)

            def merged_lo(k):
                dve.wait_ge(mh_done, k + 1)
                dve.tensor_tensor(x_lo[:, k, :], o_t[:, k, :], x_hi[:, k, :].bitcast(F32),
                                  ALU.subtract).then_inc(ml_done, 1)

            def w_out_lo(k):
                dve.wait_ge(wo_hi, k + 1)
                dve.tensor_tensor(r_lo[:, k, :], raw[:, (W_OUT + k) % 2, :], r_hi[:, k, :].bitcast(F32),
                                  ALU.subtract).then_inc(wo_lo, 1)

            for j in range(KT - 1):
                merge(j)
            for k in range(KT - 1):
                merged_lo(k)
            w_out_lo(0)
            merge(KT - 1)
            for k in range(1, KT):
                w_out_lo(k)
                if k == 2:
                    merged_lo(KT - 1)
            dve.wait_ge(ml_done, KT)
            dve.wait_ge(ln_in, 32)
            chain = 0
            for s in range(SB):
                r = o_t[:, s % 2, :]
                y = o_t[:, 2 + s % 2, :]
                st = small[:, s % 2, :]
                bn = small[:, 4 + 2 * (s % 2):6 + 2 * (s % 2), 0:6]
                dve.wait_ge(xn_in[s % 2], 16 * (s // 2 + 1))
                for h in range(2):
                    dve.wait_ge(r_psum, 2 * s + h + 1)
                    dve.scalar_tensor_tensor(out=r[:, half(h)], in0=raw[:, s % 2, half(h)], scalar=ALPHA,
                                             in1=ps[:, out_bank(s, h), :], op0=ALU.mult,
                                             op1=ALU.add).then_inc(r_set, 1)
                    dve.wait_ge(r_set, 2 * s + h + 1)
                    dve.bn_stats(bn[:, h, :], r[:, half(h)]).then_inc(ln_chain, 1)
                chain += 2
                dve.wait_ge(ln_chain, chain)
                dve.bn_aggr(st[:, 0:2], bn).then_inc(ln_var, 1)
                dve.wait_ge(ln_std, s + 1)
                dve.reciprocal(st[:, 3:4], st[:, 2:3]).then_inc(ln_chain, 1)
                chain += 1
                dve.wait_ge(ln_chain, chain)
                dve.scalar_tensor_tensor(out=st[:, 4:5], in0=st[:, 0:1], scalar=-1.0, in1=st[:, 3:4],
                                         op0=ALU.mult, op1=ALU.mult).then_inc(ln_nb, 1)
                if s >= 2:
                    dve.wait_ge(out_done[s % 2], 32 * (s // 2))
                for h in range(2):
                    dve.wait_ge(ln_norm, 2 * s + h + 1)
                    dve.tensor_tensor(y[:, half(h)], r[:, half(h)], g_bc[:, half(h)], ALU.mult).then_inc(ln_chain, 1)
                    chain += 1
                    dve.wait_ge(ln_chain, chain)
                    dve.tensor_tensor(y[:, half(h)], y[:, half(h)], b_bc[:, half(h)], ALU.add).then_inc(ln_out, 1)

        @block.tensor
        def _(pe):
            def chunk(n, q, use=None, split=False):
                use = n if use is None else use
                h, s = q // 2, n % 2
                if q == 0:
                    pe.wait_ge(lo_done, n + 1)
                if q % 2 == 0:
                    if use > USE_U:
                        pe.wait_ge(mg_sig, 2 * (use - 1 - USE_U) + h + 1)
                    elif use > 0:
                        pe.wait_ge(bank_free[h], use)
                for k in range(4 * (q % 2), 4 * (q % 2) + 4):
                    if n == 0:
                        pe.wait_ge(x_lo_done, KT * h + k + 1)
                    wk = slice(P * k, P * (k + 1))
                    xs = slice(HALF * h, HALF * (h + 1))
                    last = mma3(pe, ps[:, h, :], w_hi[:, s, wk], w_lo[:, s, wk], x_hi[:, k, xs],
                                x_lo[:, k, xs], k == 0, k == KT - 1)
                if q % 2 == 1:
                    last.then_inc(half_done, 1)

            def t_bank(i):
                if i >= 2:
                    pe.wait_ge(tp_free, i - 1)
                return ps[:, 5 + i % 2, :]

            for n in range(0, GATE_A):
                for q in range(4):
                    chunk(n, q)
                if n == Q_A:
                    pe.wait_ge(masks, 2)
                    for h in range(2):
                        pe.wait_ge(bank_free[h], V_A + 1)
                if n >= Q_A:
                    i = n - Q_A
                    bank = t_bank(i)
                    for b_ in range(4):
                        c = 4 * i + b_
                        keys = P if c < NCHUNK - 1 else CHUNK
                        last = pe.transpose(bank[0:keys, P * b_:P * (b_ + 1)],
                                            v_t[:, CHUNK * c:CHUNK * c + keys], ident[:])
                    last.then_inc(tp_done, 1)

            chunk(GATE_A, 0)
            for c in range(NCHUNK + 3):
                if 2 <= c < NCHUNK + 2:
                    i = c - 2
                    keys = P if i < NCHUNK - 1 else CHUNK
                    pe.wait_ge(za_p, i + 1)
                    bank = t_bank(4 + i)
                    for cb in range(4):
                        last = pe.transpose(bank[0:keys, P * cb:P * (cb + 1)],
                                            prob[:, i % 3, P * cb:P * cb + keys], ident[:])
                    last.then_inc(tp_done, 1)
                if c < NCHUNK:
                    if c < NCHUNK - 1:
                        chunk(GATE_A + (c + 1) // 4, (c + 1) % 4)
                    if c == 0:
                        pe.wait_ge(k_dup, 64)
                        pe.wait_ge(q_split, 16)
                    if c >= 2:
                        pe.wait_ge(za_exp, 5 * (c - 1))
                    keys = P if c < NCHUNK - 1 else CHUNK
                    for g in range(2):
                        for pr in range(2):
                            cb = 2 * g + pr
                            o = ps[:, 2 + c % 2, P * cb:P * cb + keys]
                            q_ = qa[:, g, c, 2 * pr:2 * pr + 2, :].rearrange("p a t -> p (a t)")
                            for part in range(2):
                                last = pe.matmul(o, q_, ka[:, part, g, CHUNK * c:CHUNK * c + keys],
                                                 start=part == 0, stop=part == 1)
                    last.then_inc(za_done, 1)
                if c >= 3:
                    i = c - 3
                    pe.wait_ge(tp_free, 4 + i + 1)
                    if i >= 2:
                        pe.wait_ge(oa_free, i - 1)
                    keys = P if i < NCHUNK - 1 else CHUNK
                    bank = 7 if i % 2 == 0 else 4
                    for g in range(2):
                        last = pe.matmul(ps[HD * g:HD * g + HD, bank, 0:4 * CHUNK],
                                         v_win[0:keys, i, HD * g:HD * g + HD],
                                         prob_t[0:keys, i % 2, 2 * P * g:2 * P * (g + 1)],
                                         start=True, stop=True)
                    last.then_inc(oa_done, 1)

            for n in (V_B0, GATE_B0):
                for q in range(4):
                    chunk(n, q)

            def tb_bank(i):
                if i >= 2:
                    pe.wait_ge(tb_free, i - 1)
                else:
                    pe.wait_ge(tp_free, 4 + NCHUNK)
                return ps[:, 5 + i % 2, :]

            def turn(p, k, groups):
                i = 8 * p + k
                for g in groups:
                    pe.wait_ge(w_ready, 2 * (i + 1))
                    bank = tb_bank(T_PAIR * p + 2 + T_GROUPS * k + g)
                    for b_ in range(4 * g, min(4 * g + 4, SB + 1)):
                        at = P * (b_ % 4)
                        last = pe.transpose(bank[:, at:at + P], beta[:, i % 2, P * b_:P * (b_ + 1)], ident[:])
                    last.then_inc(tb_done, 1)

            def scores(p, k):
                h, tb, n1, tb2, n2 = step(k)
                i = 8 * p + k
                if i > 0:
                    pe.wait_ge(z_free, i)
                for z, t, width in ((z_big, tb, n1), (z_small, tb2, n2)):
                    for at in range(0, width, HALF):
                        m = min(HALF, width - at)
                        for part in range(2):
                            last = pe.matmul(z[:, at:at + m], qs[:, h, P * t:P * (t + 1)],
                                             ks[:, part, h, P * t + at:P * t + at + m],
                                             start=part == 0, stop=part == 1)
                last.then_inc(z_done, 1)

            def values(p, k):
                h, tb, n1, tb2, n2 = step(k)
                i = 8 * p + k
                if i >= 1:
                    pe.wait_ge(o_free, i)
                nb1 = n1 // P
                for b_ in range(SB + 1):
                    if b_ % 4 == 0:
                        pe.wait_ge(tb_free, T_PAIR * p + 2 + T_GROUPS * k + b_ // 4 + 1)
                    small_b = b_ >= nb1
                    kb = tb2 + b_ - nb1 if small_b else tb + b_
                    last = pe.matmul(ps[:, 7, 2 * P * small_b:2 * P * (small_b + 1)],
                                     v_n[:, kb, h, :, :].rearrange("p a d -> p (a d)"),
                                     w_t[:, b_, :, :].rearrange("p a t -> p (a t)"),
                                     start=b_ in (0, nb1), stop=b_ in (nb1 - 1, SB))
                last.then_inc(o_done, 1)

            for p in range(PAIRS):
                n = LOOP_B + 4 * p
                chunk(n, 0) if p == 0 else None
                if p > 0:
                    turn(p - 1, 6, (0, 1))
                    chunk(n, 0)
                    turn(p - 1, 6, (2,))
                    values(p - 1, 6)
                chunk(n, 1)
                if p > 0:
                    turn(p - 1, 7, (0, 1))
                chunk(n, 2)
                if p > 0:
                    turn(p - 1, 7, (2,))
                    values(p - 1, 7)
                chunk(n, 3)
                for h in range(2):
                    pe.wait_ge(bank_free[h], V_B0 + 4 * p + 1)
                for g in range(2):
                    bank = tb_bank(T_PAIR * p + g)
                    for b_ in range(4 * g, 4 * g + 4):
                        last = pe.transpose(bank[:, P * (b_ % 4):P * (b_ % 4) + P], v_t[:, P * b_:P * (b_ + 1)],
                                            ident[:])
                    last.then_inc(tb_done, 1)
                for q in range(4):
                    chunk(n + 1, q)
                for k in range(8):
                    if k >= 2:
                        turn(p, k - 2, (0, 1))
                    chunk(n + 2 + k // 4, k % 4)
                    if k == 0:
                        pe.wait_ge(k_dup, 64 * (p + 2))
                        for h in range(2):
                            pe.wait_ge(bank_free[h], n + 2)
                    if k >= 2:
                        turn(p, k - 2, (2,))
                    scores(p, k)
                    if k >= 2:
                        values(p, k - 2)

            def up(j):
                n = up_tile(j)
                pe.wait_ge(lo_done, n + 1)
                if j > 0:
                    pe.wait_ge(yb_mul, 2 * j)
                s = n % 2
                for ab in range(2):
                    for h in range(2):
                        for k in range(4):
                            kk = 4 * ab + k
                            if j == 0:
                                pe.wait_ge(ol_done, kk + 1)
                            wk = slice(P * kk, P * (kk + 1))
                            xs = slice(HALF * h, HALF * (h + 1))
                            last = mma3(pe, ps[:, 2 + 2 * ab + h, :], w_hi[:, s, wk], w_lo[:, s, wk],
                                        r_hi[:, kk, xs], r_lo[:, kk, xs], k == 0, k == 3)
                last.then_inc(up_done, 1)

            for j in range(1, KT):
                n = merge_tile(j, 0)
                for q in range(4):
                    if j == 1:
                        if q < 2:
                            turn(PAIRS - 1, 6 + q, (0, 1))
                    chunk(n, q, USE_U + 2 * j)
                    if j == 1 and q < 2:
                        turn(PAIRS - 1, 6 + q, (2,))
                        values(PAIRS - 1, 6 + q)
                up(j - 1)
                for q in range(4):
                    chunk(merge_tile(j, 1), q, USE_U + 2 * j + 1)
            up(KT - 1)

            for k in range(KT):
                pe.wait_ge(ml_done, k + 1)
                pe.wait_ge(wo_lo, k + 1)
                for s in range(4):
                    if k == 0 and s == 0:
                        pe.wait_ge(mg_sig, 4 * KT)
                    if k == 0 and s == 2:
                        pe.wait_ge(yb_mul, 2 * KT)
                    for h in range(2):
                        xs, ws = slice(P * s, P * (s + 1)), slice(HALF * h, HALF * (h + 1))
                        last = mma3(pe, ps[:, out_bank(s, h), :], x_hi[:, k, xs], x_lo[:, k, xs],
                                    r_hi[:, k, ws], r_lo[:, k, ws], k == 0, k == KT - 1)
                        if k == KT - 1:
                            last.then_inc(r_psum, 1)
            for s in range(4, SB):
                for h in range(2):
                    pe.wait_ge(r_set, 2 * (s - 4) + h + 1)
                    for k in range(KT):
                        xs, ws = slice(P * s, P * (s + 1)), slice(HALF * h, HALF * (h + 1))
                        last = mma3(pe, ps[:, out_bank(s, h), :], x_hi[:, k, xs], x_lo[:, k, xs],
                                    r_hi[:, k, ws], r_lo[:, k, ws], k == 0, k == KT - 1)
                    last.then_inc(r_psum, 1)


def columns():
    at = np.cumsum([0, 512, 128, 128, 512, 512, 512, 512, 512, D, D])
    q_a, k_a, v_a, gate_a, q_b, k_b, v_b, gate_b, mg_a, mg_b = at[:-1]
    tile = np.arange(P)

    def heads(base, i):
        return np.concatenate([base + HD * (GROUP * g + i) + np.arange(HD) for g in range(2)])

    order = {K_A: k_a + tile, V_A: v_a + tile}
    for i in range(4):
        order[Q_A + i] = heads(q_a, i)
        order[GATE_A + i] = heads(gate_a, i)
    for p in range(PAIRS):
        order[V_B0 if p == 0 else LOOP_B + 4 * p - 2] = v_b + P * p + tile
        order[GATE_B0 if p == 0 else LOOP_B + 4 * p - 1] = gate_b + P * p + tile
        order[LOOP_B + 4 * p] = k_b + P * p + tile
        order[LOOP_B + 4 * p + 1] = q_b + P * p + tile
    for j in range(KT):
        order[merge_tile(j, 0)] = mg_a + P * j + tile
        order[merge_tile(j, 1)] = mg_b + P * j + tile
    return order


def kernel(x, w_in, b_in, sinks, w_up_a, w_up_b, w_out, ln_g, ln_b):
    import concourse.bacc as bacc
    from concourse.bass_utils import run_bass_kernel_spmd

    x, w_in, b_in, sinks, w_up_a, w_up_b, w_out, ln_g, ln_b = (
        np.asarray(t)[0] for t in (x, w_in, b_in, sinks, w_up_a, w_up_b, w_out, ln_g, ln_b))
    backwards = x[::-1]
    w = np.empty((N_TILES, P, D), x.dtype)
    bias = np.zeros((P, W_OUT), x.dtype)
    for n, cols in columns().items():
        w[n] = w_in[:, cols].reshape(KT, P, P).transpose(1, 0, 2).reshape(P, D)
        bias[:, n] = b_in[cols]
    up_rows = np.concatenate([HD * (GROUP * g + i) + np.arange(HD) for i in range(4) for g in range(2)])
    up = np.concatenate([w_up_a[up_rows], w_up_b])
    for j in range(KT):
        w[up_tile(j)] = up[:, P * j:P * (j + 1)].reshape(KT, P, P).transpose(1, 0, 2).reshape(P, D)
        w[W_OUT + j] = w_out[P * j:P * (j + 1)]
    sink_rows = np.repeat(sinks.reshape(2, 2, 2).transpose(2, 0, 1).reshape(2, GROUP), CHUNK, axis=0)
    half = HD // 2
    freq = np.float32(10000.0) ** (-np.arange(half, dtype=np.float32) / np.float32(half))
    angle = (freq[:, None] * np.arange(SEQ, dtype=np.float32)[None, ::-1]).astype(np.float64)
    cos = np.tile(np.cos(angle), (4, 1)).astype(np.float32)
    sin = np.tile(np.concatenate([-np.sin(angle), np.sin(angle)]), (2, 1)).astype(np.float32)
    arrays = {
        "xt": np.ascontiguousarray(backwards.T).reshape(KT, P, SEQ),
        "xn": np.ascontiguousarray(backwards).reshape(SB, P, D),
        "w": w, "bias": bias, "cos": cos, "sin": sin, "sinks": np.ascontiguousarray(sink_rows),
        "ln_g": np.ascontiguousarray(np.broadcast_to(ln_g, (P, D))),
        "ln_b": np.ascontiguousarray(np.broadcast_to(ln_b, (P, D))),
    }
    nc = bacc.Bacc("TRN2", target_bir_lowering=False, num_devices=1)
    args = [nc.dram_tensor(f"in_{k}", a.shape, mybir.dt.from_np(a.dtype), kind="ExternalInput").ap()
            for k, a in arrays.items()]
    out = nc.dram_tensor("out_0", (SB, P, D), F32, kind="ExternalOutput").ap()
    build(nc, *args, out)
    r = run_bass_kernel_spmd(nc, [{f"in_{k}": a for k, a in arrays.items()}], core_ids=[0])
    return r.results[0]["out_0"].reshape(SEQ, D)[::-1].reshape(1, SEQ, D)
```

```python
from contextlib import ExitStack

import numpy as np

import concourse.bass as bass
from concourse import mybir

F32 = mybir.dt.float32
F32R = mybir.dt.float32r
ACT = mybir.ActivationFunctionType
ALU = mybir.AluOpType
AX_X = mybir.AxisListType.X

P = 128
SEQ = 1024
D = 1024
HD = 64
KT = D // P
SB = SEQ // P
HALF = 512
CHUNK = 64
NCHUNK = SEQ // CHUNK
GROUP = 4
PAIRS = 4
SCALE = HD ** -0.5
ALPHA = 2.0 ** 0.25
LN_EPS = 1e-5

K_A, V_A, Q_A, GATE_A = 0, 1, 2, 6
V_B0, GATE_B0, LOOP_B = 10, 11, 12
MG_0 = LOOP_B + 4 * PAIRS - 2
LOOP_U = MG_0 + 2
W_OUT = MG_0 + 3 * KT
N_TILES = W_OUT + KT
WARM_UP = 16
EARLY = 3
ROPE_HI = 4 * (1 + GATE_A - Q_A)
USE_U = MG_0
STEP_COLS = SEQ + P
T_GROUPS = 3
T_PAIR = 2 + 8 * T_GROUPS


def up_tile(j):
    return LOOP_U + 3 * j + 1 if j < KT - 1 else W_OUT - 1


def halves_done(n, h):
    return 2 * h + n + 1 if n <= V_A else 2 * n + h + 1


def merge_tile(j, ab):
    return MG_0 + ab if j == 0 else LOOP_U + 3 * (j - 1) + 2 * ab


def out_bank(s, h):
    return (0, 6, 2, 4)[s % 4] + h


def mma3(pe, out, w_hi, w_lo, x_hi, x_lo, first, last):
    pe.matmul(out, w_hi, x_hi, start=first, stop=False)
    pe.matmul(out, w_hi, x_lo, start=False, stop=False)
    return pe.matmul(out, w_lo, x_hi, start=False, stop=last)


def build(nc, xt, xn, w, bias, cos, sin, sinks, ln_g, ln_b, out):
    with ExitStack() as ctx:
        def sb(name, shape, dt=F32, where=ctx):
            return where.enter_context(nc.sbuf_tensor(name, shape, dt))

        def sem(name):
            return ctx.enter_context(nc.semaphore(name))

        x_hi = sb("x_hi", [P, KT, SEQ], F32R)
        x_lo = sb("x_lo", [P, KT, SEQ], F32R)
        raw = sb("raw", [P, 2, D])
        w_hi = sb("w_hi", [P, 2, D], F32R)
        w_lo = sb("w_lo", [P, 2, D], F32R)
        o_t = sb("o_t", [P, KT, SEQ])
        v_t = sb("v_t", [P, SEQ])
        ident = sb("ident", [P, P])
        later = sb("later", [P, P])
        bias_c = sb("bias_c", [P, W_OUT])
        sink_c = sb("sink_c", [P, GROUP])
        nsink_c = sb("nsink_c", [P, GROUP])
        small = sb("small", [P, 8, 8])
        eps_c = sb("eps_c", [P, 1])
        sig_m = sb("sig_m", [P, 6, HALF])
        sig_g = sig_m[:, 2, :]
        o_part = sig_m[:, 3, :]
        cos_t, sin_t = o_t[:, 0, :], o_t[:, 1, :]
        ps = ctx.enter_context(nc.psum_tensor("ps", [P, 8, HALF], F32))

        x_in = [sem(f"x_in{k}") for k in range(2 * KT)]
        raw_in = [sem(f"raw_in{i}") for i in range(2)]
        const_in = sem("const_in")
        first_in = [sem(f"first_in{i}") for i in range(2)]
        first_hi, first_lo = sem("first_hi"), sem("first_lo")
        rope_in = sem("rope_in")
        ln_in = sem("ln_in")
        xn_in = [sem(f"xn_in{i}") for i in range(2)]
        k_dup = sem("k_dup")
        out_done = [sem(f"out_done{i}") for i in range(2)]
        masks = sem("masks")
        eps_set = sem("eps_set")
        ones_set, sink_set, stick_ones = sem("ones_set"), sem("sink_set"), sem("stick_ones")
        x_hi_done, x_lo_done = sem("x_hi_done"), sem("x_lo_done")
        hi_done, lo_first, lo_done = sem("hi_done"), sem("lo_first"), sem("lo_done")
        half_done = sem("half_done")
        bank_free = [sem("bank_free0"), sem("bank_free1")]
        swapped = sem("swapped")
        dve_rope = sem("dve_rope")
        rope_done = sem("rope_done")
        split_hi = sem("split_hi")
        k_split = sem("k_split")
        q_split = sem("q_split")
        gate_set = sem("gate_set")
        tp_done, tp_free = sem("tp_done"), sem("tp_free")
        tb_done, tb_hi, tb_free = sem("tb_done"), sem("tb_hi"), sem("tb_free")
        o_copied, o_summed, o_set = sem("o_copied"), sem("o_summed"), sem("o_set")
        za_done, za_max, za_bias, za_exp, za_sum, za_p = (
            sem("za_done"), sem("za_max"), sem("za_bias"), sem("za_exp"), sem("za_sum"), sem("za_p"))
        oa_done, oa_free = sem("oa_done"), sem("oa_free")
        ga_sig, ga_mul, ga_set = sem("ga_sig"), sem("ga_mul"), sem("ga_set")
        z_done, za_free, zb_free = sem("z_done"), sem("za_free"), sem("zb_free")
        masked, kept, scanned, w_ready = sem("masked"), sem("kept"), sem("scanned"), sem("w_ready")
        o_done, o_free = sem("o_done"), sem("o_free")
        oh_done, ol_done = sem("oh_done"), sem("ol_done")
        up_done, mg_sig, ya_mul, yb_mul, m_set = (
            sem("up_done"), sem("mg_sig"), sem("ya_mul"), sem("yb_mul"), sem("m_set"))
        mh_done, ml_done, wo_hi, wo_lo = sem("mh_done"), sem("ml_done"), sem("wo_hi"), sem("wo_lo")
        r_psum, r_set, ln_chain, ln_var, ln_std, ln_nb, ln_norm, ln_out = (
            sem("r_psum"), sem("r_set"), sem("ln_chain"), sem("ln_var"), sem("ln_std"),
            sem("ln_nb"), sem("ln_norm"), sem("ln_out"))
        ln_gain, ln_last = sem("ln_gain"), sem("ln_last")

        with ExitStack() as a:
            qa = sb("qa", [P, 2, NCHUNK, GROUP, CHUNK], F32R, a)
            ka = sb("ka", [P, 2, 2, SEQ], F32R, a)
            v_win = sb("v_win", [P, NCHUNK, P], F32, a)
            prob = sb("prob", [P, 3, HALF], F32, a)
            prob_t = sb("prob_t", [P, 2, HALF], F32, a)
        with ExitStack() as b:
            qs = sb("qs", [P, 2, SEQ], F32R, b)
            ks = sb("ks", [P, 2, 2, SEQ], F32R, b)
            v_n = sb("v_n", [P, SB, 2, 2, HD], F32R, b)
            beta = sb("beta", [P, 2, STEP_COLS], F32, b)
            keep = sb("keep", [P, 2, STEP_COLS], F32, b)
            stick_a = sb("stick_a", [P, SEQ + 1], F32, b)
            stick_b = sb("stick_b", [P, HALF + 1], F32, b)
            w_t = sb("w_t", [P, SB + 1, 2, P], F32R, b)
        with ExitStack() as u:
            r_t = sb("r_t", [P, KT, 2, SEQ], F32R, u)
            r_hi, r_lo = r_t[:, :, 0, :], r_t[:, :, 1, :]
        g_bc = sig_m[:, 0:2, :].rearrange("p a b -> p (a b)")
        b_bc = sig_m[:, 2:4, :].rearrange("p a b -> p (a b)")

        block = ctx.enter_context(nc.Block())
        z_big = ps[:, 2:4, :].rearrange("p a b -> p (a b)")
        z_small = ps[:, 4, :]

        def step(k):
            h, j = k % 2, k // 2
            return h, j, SEQ - P * j, SB - 1 - j, P * (j + 1)

        @block.sync
        def _(sp):
            def load_w(n):
                if n >= 2:
                    if n - 2 <= W_OUT:
                        sp.wait_ge(lo_done, n - 1)
                    else:
                        sp.wait_ge(wo_lo, n - 2 - W_OUT)
                sp.dma_start(raw[:, n % 2, :], w[n]).then_inc(raw_in[n % 2], 16)

            def duplicate_keys(keys):
                for part in range(2):
                    for g in range(2):
                        have, want = slice(HD * g, HD * g + HD), slice(HD - HD * g, P - HD * g)
                        sp.dma_start(keys[want, part, g, :].bitcast(F32),
                                     keys[have, part, g, :].bitcast(F32)).then_inc(k_dup, 16)

            sp.dma_start(raw[:, 0, 0:HALF], w[0][:, 0:HALF]).then_inc(first_in[0], 16)
            for h in range(2):
                cols = slice(HALF * h, HALF * (h + 1))
                for k in range(KT):
                    if h == 0 and k == 2:
                        sp.dma_start(raw[:, 0, HALF:D], w[0][:, HALF:D]).then_inc(raw_in[0], 16)
                    sp.dma_start(o_t[:, k, cols], xt[k][:, cols]).then_inc(x_in[KT * h + k], 16)
                if h == 0:
                    sp.dma_start(raw[:, 1, 0:HALF], w[1][:, 0:HALF]).then_inc(first_in[1], 16)
                    sp.dma_start(raw[:, 1, HALF:D], w[1][:, HALF:D]).then_inc(raw_in[1], 16)
                    for dst, src in ((bias_c, bias), (sink_c, sinks)):
                        sp.dma_start(dst[:], src).then_inc(const_in, 16)
            load_w(2)
            sp.wait_ge(x_lo_done, KT + 2)
            sp.dma_start(cos_t, cos).then_inc(rope_in, 16)
            sp.dma_start(sin_t, sin).then_inc(rope_in, 16)
            load_w(3)
            for n in range(4, LOOP_B + 4):
                if n == 5:
                    sp.wait_ge(k_split, 4)
                    duplicate_keys(ka)
                load_w(n)
            for p in range(PAIRS):
                sp.wait_ge(bank_free[0], LOOP_B + 4 * p + 1)
                sp.wait_ge(bank_free[1], LOOP_B + 4 * p + 1)
                duplicate_keys(ks)
                if p < PAIRS - 1:
                    for i in range(4):
                        load_w(LOOP_B + 4 * (p + 1) + i)
            for n in range(LOOP_B + 4 * PAIRS, N_TILES):
                load_w(n)
            sp.wait_ge(m_set, 2 * KT)
            sp.dma_start(g_bc, ln_g).then_inc(ln_in, 16)
            sp.dma_start(b_bc, ln_b).then_inc(ln_in, 16)
            sp.wait_ge(wo_lo, KT - 1)

            def store_rows(s):
                for h in range(2):
                    cols = slice(HALF * h, HALF * (h + 1))
                    if s < SB - 1:
                        sp.wait_ge(ln_out, 2 * s + h + 1)
                    else:
                        sp.wait_ge(ln_last, h + 1)
                    sp.dma_start(out[s][:, cols], o_t[:, 2 + s % 2, cols]).then_inc(out_done[s % 2], 16)

            for s in range(SB):
                if s >= 2:
                    sp.wait_ge(r_set, 2 * (s - 1))
                sp.dma_start(raw[:, s % 2, :], xn[s]).then_inc(xn_in[s % 2], 16)
                if s >= 2:
                    store_rows(s - 2)
            store_rows(SB - 2)
            store_rows(SB - 1)
            sp.wait_ge(out_done[0], 32 * (SB // 2))
            sp.wait_ge(out_done[1], 32 * (SB // 2))

        @block.gpsimd
        def _(pool):
            pool.memset(ident[:], 0.0).then_inc(ones_set, 1)
            pool.memset(later[:], 1.0).then_inc(ones_set, 1)
            pool.wait_ge(ones_set, 2)
            pool.affine_select(out=ident[:], in_=ident[:], compare_op=ALU.not_equal, fill=1.0, base=0,
                               pattern=[[-1, P]], channel_multiplier=1).then_inc(masks, 1)
            pool.affine_select(out=later[:], in_=later[:], compare_op=ALU.is_gt, fill=0.0, base=0,
                               pattern=[[1, P]], channel_multiplier=-1).then_inc(masks, 1)

            def low_weights(n, parts=None):
                pool.wait_ge(hi_done, n + 1)
                for part in parts or (None,):
                    cols = slice(0, D) if part is None else slice(HALF * part, HALF * (part + 1))
                    pool.tensor_tensor(w_lo[:, n % 2, cols], raw[:, n % 2, cols],
                                       w_hi[:, n % 2, cols].bitcast(F32),
                                       ALU.subtract).then_inc(lo_first if part == 0 else lo_done, 1)

            def gate_product(p, h):
                cols = slice(HALF * h, HALF * (h + 1))
                pool.wait_ge(bank_free[h], GATE_B0 + 4 * p + 1)
                o = o_t[:, 4 + p, cols]
                pool.tensor_tensor(o, o, sig_g[:], ALU.mult).then_inc(gate_set, 1)

            def keeps(p, k, q):
                h, tb, n1, tb2, n2 = step(k)
                i = 8 * p + k
                at, m = ((0, n1), (n1, n2))[q]
                bt = beta[:, i % 2, at:at + m]
                pool.wait_ge((za_free, zb_free)[q], i + 1)
                pool.tensor_tensor(bt[:, 0:P], bt[:, 0:P], later[:], ALU.mult).then_inc(masked, 1)
                pool.wait_ge(masked, 2 * i + q + 1)
                if i >= 2:
                    pool.wait_ge(scanned, 2 * (i - 1))
                pool.tensor_scalar(keep[:, i % 2, at:at + m], bt, -1.0, 1.0, ALU.mult, ALU.add).then_inc(kept, 1)

            def store_out(p, k):
                h, tb, n1, tb2, n2 = step(k)
                i = 8 * p + k
                r = slice(HD * h, HD * h + HD)
                pool.wait_ge(o_free, i + 1)
                both = o_part[r, :].rearrange("p (q s t) -> p q s t", q=2, s=2)
                pool.tensor_tensor(both[:, :, 0, :], both[:, :, 0, :], both[:, :, 1, :],
                                  ALU.add).then_inc(o_summed, 1)
                pool.wait_ge(o_summed, i + 1)
                for q, t in ((0, tb), (1, tb2)):
                    o = o_t[r, 4 + p, P * t:P * (t + 1)]
                    pool.tensor_tensor(o, o, both[:, q, 0, :], ALU.mult).then_inc(o_set, 1)
                pool.wait_ge(o_set, 2 * (i + 1))

            pool.wait_ge(lo_done, 2)
            for n in range(2, LOOP_B + 1):
                low_weights(n)
            for h in range(2):
                gate_product(0, h)
            low_weights(LOOP_B + 1)
            pool.wait_ge(masks, 2)
            for p in range(PAIRS):
                n = LOOP_B + 4 * p
                if p > 0:
                    for k in range(5, 8):
                        store_out(p - 1, k)
                low_weights(n + 2)
                low_weights(n + 3)
                for k in range(8):
                    if k in (4, 5):
                        low_weights(n + 4, (k - 4,))
                    if k == 6 and p < PAIRS - 1:
                        gate_product(p + 1, 0)
                    keeps(p, k, 0)
                    keeps(p, k, 1)
                    if k >= 3:
                        pool.wait_ge(kept, 2 * (8 * p + k + 1))
                        if k == 3:
                            pool.wait_ge(gate_set, 2 * (p + 1))
                        if k == 4:
                            pool.wait_ge(lo_first, p + 1)
                        if k == 5:
                            pool.wait_ge(lo_done, n + 5)
                        if k == 6 and p < PAIRS - 1:
                            pool.wait_ge(gate_set, 2 * p + 3)
                        store_out(p, k - 3)
                if p < PAIRS - 1:
                    gate_product(p + 1, 1)
                low_weights(n + 5)
                pool.wait_ge(lo_done, n + 6)
            for k in range(5, 8):
                store_out(PAIRS - 1, k)
            for n in range(LOOP_B + 4 * PAIRS + 2, W_OUT + 1):
                low_weights(n)
            pool.wait_ge(ln_in, 32)
            for s in range(SB - 1):
                if s >= 2:
                    pool.wait_ge(out_done[s % 2], 32 * (s // 2))
                for h in range(2):
                    cols = slice(HALF * h, HALF * (h + 1))
                    y = o_t[:, 2 + s % 2, cols]
                    pool.wait_ge(ln_norm, 2 * s + h + 1)
                    pool.tensor_tensor(y, o_t[:, s % 2, cols], g_bc[:, cols], ALU.mult).then_inc(ln_gain, 1)
                    pool.wait_ge(ln_gain, 2 * s + h + 1)
                    pool.tensor_tensor(y, y, b_bc[:, cols], ALU.add).then_inc(ln_out, 1)

        @block.scalar
        def _(act):
            def tile_used(n):
                j, i = divmod(n - LOOP_U, 3)
                if n < LOOP_U:
                    act.wait_ge(half_done, halves_done(n, 1))
                elif i == 1:
                    act.wait_ge(up_done, j + 1)
                else:
                    act.wait_ge(half_done, 2 * (USE_U + 2 * (j + 1) + i // 2) + 2)

            def weight_hi(n):
                act.wait_ge(raw_in[n % 2], 16 * (n // 2 + 1))
                if n >= 2:
                    tile_used(n - 2)
                act.activation(w_hi[:, n % 2, :], raw[:, n % 2, :], ACT.Copy).then_inc(hi_done, 1)

            def half(h):
                return slice(HALF * h, HALF * (h + 1))

            def b_of(n, lo=0, hi=P):
                return bias_c[lo:hi, n:n + 1]

            def rope_index(n, h):
                return 2 * (n if n == K_A else n - 1) + h

            def rope_swap(n, h):
                i = rope_index(n, h)
                act.wait_ge(half_done, halves_done(n, h))
                if i >= 2:
                    act.wait_ge(rope_done, i - 1)
                for q in range(4):
                    o = 32 * (q ^ 1)
                    act.activation(sig_m[o:o + 32, i % 2, :], ps[32 * q:32 * q + 32, h, :], ACT.Identity,
                                   bias=b_of(n, 32 * q, 32 * q + 32)).then_inc(swapped, 1)

            def rope_hi(n, h):
                i = rope_index(n, h)
                act.wait_ge(rope_done, i + 1)
                for g in range(2):
                    r = slice(HD * g, HD * g + HD)
                    rot = sig_m[r, 2 + i % 2, :]
                    if n == K_A:
                        dst, src = ka[r, 0, g, half(h)], rot
                    else:
                        dst = qa[r, g, 8 * h:8 * h + 8, n - Q_A, :]
                        src = rot.rearrange("p (c t) -> p c t", t=CHUNK)
                    act.activation(dst, src, ACT.Copy).then_inc(split_hi, 1)

            def head_hi(n, h, dst):
                act.wait_ge(half_done, 2 * n + h + 1)
                for g in range(2):
                    r = slice(HD * g, HD * g + HD)
                    act.activation(dst[r, g, half(h)], ps[r, h, :], ACT.Identity,
                                   bias=b_of(n, HD * g, HD * g + HD)).then_inc(split_hi, 1)

            def value_half(n, h):
                act.wait_ge(half_done, halves_done(n, h))
                if n == V_A:
                    act.wait_ge(bank_free[h], 1)
                act.activation(v_t[:, half(h)], ps[:, 2 + h if n == V_A else h, :], ACT.Identity,
                               bias=b_of(n)).then_inc(bank_free[h], 1)

            def gate_b_half(n, h):
                p = (n - GATE_B0) // 4
                act.wait_ge(half_done, 2 * n + h + 1)
                if p == 0:
                    act.wait_ge(ga_set, 1)
                act.activation(o_t[:, 4 + p, half(h)], ps[:, h, :], ACT.Identity, bias=b_of(n))
                if 2 * p + h > 0:
                    act.wait_ge(gate_set, 2 * p + h)
                act.activation(sig_g[:], ps[:, h, :], ACT.Sigmoid, bias=b_of(n)).then_inc(bank_free[h], 1)

            def first_weights_hi(n, h):
                act.wait_ge((raw_in if h else first_in)[n], 16)
                act.activation(w_hi[:, n, half(h)], raw[:, n, half(h)],
                               ACT.Copy).then_inc(hi_done if h else first_hi, 1)

            first_weights_hi(0, 0)
            for h in range(2):
                for k in range(KT):
                    if h == 0 and k == 2:
                        first_weights_hi(0, 1)
                    act.wait_ge(x_in[KT * h + k], 16)
                    act.activation(x_hi[:, k, half(h)], o_t[:, k, half(h)], ACT.Copy).then_inc(x_hi_done, 1)
                if h == 0:
                    first_weights_hi(1, 0)
                    first_weights_hi(1, 1)
            act.wait_ge(const_in, 32)
            def window_group(i):
                act.wait_ge(tp_done, i + 1)
                src = ps[:, 5 + i % 2, :]
                full = 4 if i < 3 else 3
                ins = act.activation(v_win[:, 4 * i:4 * i + full, :].rearrange("p a b -> p (a b)"),
                                     src[:, 0:P * full], ACT.Copy)
                if i == 3:
                    ins = act.activation(v_win[0:CHUNK, NCHUNK - 1, :],
                                         src[0:CHUNK, P * 3:P * 4], ACT.Copy)
                ins.then_inc(tp_free, 1)

            before = None
            for h in range(2):
                if h == 1:
                    weight_hi(Q_A)
                rope_swap(K_A, h)
                value_half(V_A, h)
                rope_hi(K_A, h)
            weight_hi(Q_A + 1)
            for n in range(Q_A, GATE_A):
                if n > Q_A:
                    window_group(n - Q_A - 1)
                for h in range(2):
                    rope_swap(n, h)
                    if before:
                        rope_hi(*before)
                    before = (n, h)
                weight_hi(n + 2)
            rope_hi(*before)
            window_group(3)
            for c in range(NCHUNK + 2):
                if c >= 2:
                    i = c - 2
                    rows = P if i < NCHUNK - 1 else CHUNK
                    act.wait_ge(tp_done, 4 + i + 1)
                    if i >= 2:
                        act.wait_ge(oa_done, i - 1)
                    act.activation(prob_t[0:rows, i % 2, :], ps[0:rows, 5 + i % 2, :],
                                   ACT.Copy).then_inc(tp_free, 1)
                if c < NCHUNK:
                    if c % 2 == 0:
                        n, h = GATE_A + c // 4, (c % 4) // 2
                        act.wait_ge(half_done, 2 * n + h + 1)
                        act.activation(o_t[:, 4 + c // 4, half(h)], ps[:, h, :], ACT.Identity,
                                       bias=b_of(n)).then_inc(bank_free[h], 1)
                    if c % 4 == 3:
                        weight_hi(GATE_A + c // 4 + 2)
                    keys = P if c < NCHUNK - 1 else CHUNK
                    act.wait_ge(za_bias, 2 * (c + 1))
                    sm = small[:, c % 2 * 3:c % 2 * 3 + 3, :]
                    act.activation(sm[:, 2, 0:4], sm[:, 1, 0:4], ACT.Exp).then_inc(za_exp, 1)
                    for cb in range(4):
                        act.activation(prob[:, c % 3, P * cb:P * cb + keys],
                                       ps[:, 2 + c % 2, P * cb:P * cb + keys], ACT.Exp,
                                       bias=sm[:, 0, cb:cb + 1], scale=SCALE,
                                       accum_out=sm[:, 2, 4 + cb:5 + cb]).then_inc(za_exp, 1)
            value_half(V_B0, 0)
            value_half(V_B0, 1)
            weight_hi(V_B0 + 2)
            act.wait_ge(oa_free, NCHUNK)

            def gate_a_sigmoid(i):
                if i >= 2:
                    act.wait_ge(ga_set, i - 1)
                act.activation(beta[:, i % 2, 0:SEQ], o_t[:, 4 + i, :], ACT.Sigmoid).then_inc(ga_sig, 1)

            gate_a_sigmoid(0)
            gate_a_sigmoid(1)
            gate_b_half(GATE_B0, 0)
            gate_a_sigmoid(2)
            gate_b_half(GATE_B0, 1)
            weight_hi(GATE_B0 + 2)
            gate_a_sigmoid(3)

            def turned_hi(p, k, groups):
                for g in groups:
                    i = T_PAIR * p + 2 + T_GROUPS * k + g
                    nb = 4 if g < 2 else 1
                    act.wait_ge(tb_done, i + 1)
                    act.activation(w_t[:, 4 * g:4 * g + nb, 0, :],
                                   ps[:, 5 + i % 2, 0:P * nb].rearrange("p (a t) -> p a t", t=P),
                                   ACT.Copy).then_inc(tb_hi, 1)

            def values_hi(p):
                for g in range(2):
                    i = T_PAIR * p + g
                    act.wait_ge(tb_done, i + 1)
                    act.activation(v_n[:, 4 * g:4 * g + 4, :, 0, :],
                                   ps[:, 5 + i % 2, :].rearrange("p (a h d) -> p a h d", h=2, d=HD),
                                   ACT.Copy).then_inc(tb_hi, 1)

            def betas(p, k, q):
                h, tb, n1, tb2, n2 = step(k)
                i = 8 * p + k
                act.wait_ge(z_done, i + 1)
                dst = beta[:, i % 2, :]
                if i == 0:
                    act.wait_ge(ga_set, 4)
                if q == 0:
                    act.activation(dst[:, 0:n1], z_big[:, 0:n1], ACT.Sigmoid, scale=SCALE).then_inc(za_free, 1)
                else:
                    act.activation(dst[:, n1:n1 + n2], z_small[:, 0:n2], ACT.Sigmoid,
                                   scale=SCALE).then_inc(zb_free, 1)

            def copy_out(p, k):
                h = k % 2
                i = 8 * p + k
                act.wait_ge(o_done, i + 1)
                if i >= 1:
                    act.wait_ge(o_set, 2 * i)
                act.activation(o_part[HD * h:HD * h + HD, :], ps[HD - HD * h:P - HD * h, 7, :],
                               ACT.Copy).then_inc(o_copied, 1)

            def merge_gate(j, ab, h):
                act.wait_ge(half_done, 2 * (USE_U + 2 * j + ab) + h + 1)
                if ab == 0 and j >= 2:
                    act.wait_ge(m_set, 2 * (j - 2) + h + 1)
                if ab == 1 and j >= 1:
                    act.wait_ge(m_set, 2 * (j - 1) + h + 1)
                act.activation(sig_m[:, 4 * ab + (2 * (j % 2) if ab == 0 else 0) + h, :], ps[:, h, :],
                               ACT.Sigmoid, bias=b_of(merge_tile(j, ab))).then_inc(mg_sig, 1)

            for p in range(PAIRS):
                n = LOOP_B + 4 * p
                last = p == PAIRS - 1
                if p > 0:
                    turned_hi(p - 1, 6, (0, 1))
                    copy_out(p - 1, 5)
                    weight_hi(n + 1)
                    turned_hi(p - 1, 6, (2,))
                    head_hi(n, 0, ks[:, 0])
                    turned_hi(p - 1, 7, (0, 1))
                    copy_out(p - 1, 6)
                    turned_hi(p - 1, 7, (2,))
                else:
                    head_hi(n, 0, ks[:, 0])
                head_hi(n, 1, ks[:, 0])
                weight_hi(n + 2)
                if p > 0:
                    copy_out(p - 1, 7)
                values_hi(p)
                head_hi(n + 1, 0, qs)
                head_hi(n + 1, 1, qs)
                weight_hi(n + 3)
                for k in range(8):
                    if k >= 2:
                        turned_hi(p, k - 2, (0, 1))
                    if k >= 2:
                        betas(p, k, 0)
                    if k >= 3:
                        copy_out(p, k - 3)
                    if k in (1, 4):
                        if last:
                            merge_gate(0, 0, k // 4)
                        else:
                            value_half(n + 2, k // 4)
                    if k in (5, 7):
                        if last:
                            merge_gate(0, 1, (k - 5) // 2)
                        else:
                            gate_b_half(n + 3, (k - 5) // 2)
                    if k == 3:
                        weight_hi(n + 4)
                    if k >= 2:
                        turned_hi(p, k - 2, (2,))
                    if k < 2:
                        betas(p, k, 0)
                    betas(p, k, 1)

            def branch_hi(k):
                act.activation(r_hi[:, k, :], o_t[:, k, :], ACT.Copy).then_inc(oh_done, 1)

            turned_hi(PAIRS - 1, 6, (0, 1))
            copy_out(PAIRS - 1, 5)
            weight_hi(LOOP_U + 1)
            turned_hi(PAIRS - 1, 6, (2,))
            act.wait_ge(z_done, 8 * PAIRS)
            for k in range(EARLY):
                branch_hi(k)
            turned_hi(PAIRS - 1, 7, (0, 1))
            copy_out(PAIRS - 1, 6)
            turned_hi(PAIRS - 1, 7, (2,))
            copy_out(PAIRS - 1, 7)
            for k in range(EARLY, KT):
                if k == KT - 1:
                    act.wait_ge(o_set, 16 * PAIRS)
                branch_hi(k)
            for j in range(1, KT):
                n = LOOP_U + 3 * (j - 1)
                weight_hi(n + 2)
                for h in range(2):
                    merge_gate(j, 0, h)
                weight_hi(n + 3)
                for h in range(2):
                    merge_gate(j, 1, h)
                weight_hi(n + 4)
            def merged_hi(k):
                act.activation(x_hi[:, k, :], o_t[:, k, :], ACT.Copy).then_inc(mh_done, 1)

            def w_out_hi(k):
                n = W_OUT + k
                act.wait_ge(raw_in[n % 2], 16 * (n // 2 + 1))
                act.activation(r_hi[:, k, :], raw[:, n % 2, :], ACT.Copy).then_inc(wo_hi, 1)

            act.wait_ge(m_set, 2 * (KT - 1))
            merged_hi(0)
            merged_hi(1)
            act.wait_ge(up_done, KT)
            for k in range(1, KT):
                if k + 1 == KT - 1:
                    act.wait_ge(m_set, 2 * KT)
                w_out_hi(k)
                if k + 1 < KT:
                    merged_hi(k + 1)
            for s in range(SB):
                act.wait_ge(ln_var, s + 1)
                st = small[:, s % 2, :]
                act.activation(st[:, 2:3], st[:, 1:2], ACT.Sqrt, bias=eps_c[:, 0:1]).then_inc(ln_std, 1)
                if s == SB - 1:
                    break
                act.wait_ge(ln_nb, s + 1)
                for h in range(2):
                    act.activation(o_t[:, s % 2, half(h)], o_t[:, s % 2, half(h)], ACT.Identity,
                                   bias=st[:, 4:5], scale=st[:, 3:4]).then_inc(ln_norm, 1)

        @block.vector
        def _(dve):
            def half(h):
                return slice(HALF * h, HALF * (h + 1))

            def b_of(n, lo=0, hi=P):
                return bias_c[lo:hi, n:n + 1]

            def rope_index(n, h):
                return 2 * (n if n == K_A else n - 1) + h

            def rotate(n, h):
                i = rope_index(n, h)
                t_swap, t_rot, t_cos = (sig_m[:, 2 * q + i % 2, :] for q in range(3))
                dve.wait_ge(swapped, 4 * (i + 1))
                if i >= 2:
                    dve.wait_ge(rope_done, i - 1)
                dve.scalar_tensor_tensor(out=t_cos, in0=ps[:, h, :], scalar=b_of(n), in1=cos_t[:, half(h)],
                                         op0=ALU.add, op1=ALU.mult).then_inc(bank_free[h], 1)
                dve.tensor_tensor(t_swap, t_swap, sin_t[:, half(h)], ALU.mult).then_inc(dve_rope, 1)
                dve.wait_ge(bank_free[h], n + 1)
                dve.wait_ge(dve_rope, i + 1)
                if i >= 2:
                    dve.wait_ge(split_hi, 2 * (i - 1))
                dve.tensor_tensor(t_rot, t_cos, t_swap, ALU.add).then_inc(rope_done, 1)

            def rope_lo(n, h):
                i = rope_index(n, h)
                dve.wait_ge(rope_done, i + 1)
                for g in range(2):
                    r = slice(HD * g, HD * g + HD)
                    o = slice(HD - HD * g, P - HD * g)
                    rot = sig_m[r, 2 + i % 2, :]
                    dve.wait_ge(split_hi, 2 * i + g + 1)
                    if n == K_A:
                        dve.tensor_tensor(ka[r, 1, g, half(h)], rot, ka[r, 0, g, half(h)].bitcast(F32),
                                          ALU.subtract).then_inc(k_split, 1)
                    else:
                        dve.tensor_tensor(
                            qa[o, g, 8 * h:8 * h + 8, n - Q_A, :], rot.rearrange("p (c t) -> p c t", t=CHUNK),
                            qa[r, g, 8 * h:8 * h + 8, n - Q_A, :].bitcast(F32),
                            ALU.subtract).then_inc(q_split, 1)

            def head_lo(p, n, h, dst, is_key):
                i = ROPE_HI + 8 * p + (0 if is_key else 4) + 2 * h
                for g in range(2):
                    dve.wait_ge(split_hi, i + g + 1)
                    r = slice(HD * g, HD * g + HD)
                    o = slice(HD - HD * g, P - HD * g)
                    if is_key:
                        hi_part, to = dst[r, 0, g, half(h)], dst[r, 1, g, half(h)]
                    else:
                        hi_part, to = dst[r, g, half(h)], dst[o, g, half(h)]
                    ins = dve.scalar_tensor_tensor(out=to, in0=ps[r, h, :], scalar=b_of(n, HD * g, HD * g + HD),
                                                   in1=hi_part.bitcast(F32), op0=ALU.add, op1=ALU.subtract)
                ins.then_inc(bank_free[h], 1)

            dve.memset(eps_c[:], LN_EPS).then_inc(eps_set, 1)
            def first_weights_lo(n, h):
                dve.wait_ge(hi_done if h else first_hi, n + 1)
                dve.tensor_tensor(w_lo[:, n, half(h)], raw[:, n, half(h)], w_hi[:, n, half(h)].bitcast(F32),
                                  ALU.subtract).then_inc(lo_done if h else first_lo, 1)

            first_weights_lo(0, 0)
            for h in range(2):
                for k in range(KT):
                    if h == 0 and k == 2:
                        first_weights_lo(0, 1)
                    dve.wait_ge(x_hi_done, KT * h + k + 1)
                    dve.tensor_tensor(x_lo[:, k, half(h)], o_t[:, k, half(h)], x_hi[:, k, half(h)].bitcast(F32),
                                      ALU.subtract).then_inc(x_lo_done, 1)
                if h == 0:
                    first_weights_lo(1, 0)
                    first_weights_lo(1, 1)
            dve.wait_ge(const_in, 32)
            dve.tensor_scalar(nsink_c[:], sink_c[:], -1.0, None, ALU.mult).then_inc(sink_set, 1)
            dve.wait_ge(rope_in, 32)
            before = None
            for n in range(0, GATE_A):
                if n != V_A:
                    for h in range(2):
                        rotate(n, h)
                        if before:
                            rope_lo(*before)
                        before = (n, h)
            rope_lo(*before)

            def prob_norm(c):
                keys = P if c < NCHUNK - 1 else CHUNK
                sm = small[:, c % 2 * 3:c % 2 * 3 + 3, :]
                dve.wait_ge(za_exp, 5 * (c + 1))
                dve.tensor_tensor(sm[:, 2, 0:4], sm[:, 2, 0:4], sm[:, 2, 4:8], ALU.add).then_inc(za_sum, 1)
                dve.wait_ge(za_sum, 2 * c + 1)
                dve.reciprocal(sm[:, 2, 0:4], sm[:, 2, 0:4]).then_inc(za_sum, 1)
                dve.wait_ge(za_sum, 2 * c + 2)
                pr = prob[:, c % 3, :].rearrange("p (a k) -> p a k", k=P)[:, :, 0:keys]
                dve.tensor_tensor(pr, pr, sm[:, 2, 0:4].unsqueeze(2).to_broadcast([P, 4, keys]),
                                  ALU.mult).then_inc(za_p, 1)

            dve.wait_ge(sink_set, 1)
            for c in range(NCHUNK + 3):
                if 1 <= c <= NCHUNK:
                    prob_norm(c - 1)
                if c < NCHUNK:
                    keys = P if c < NCHUNK - 1 else CHUNK
                    sm = small[:, c % 2 * 3:c % 2 * 3 + 3, :]
                    dve.wait_ge(za_done, c + 1)
                    z = ps[:, 2 + c % 2, :].rearrange("p (a k) -> p a k", k=P)[:, :, 0:keys]
                    dve.tensor_reduce(sm[:, 0, 4:8], z, AX_X, ALU.max).then_inc(za_max, 1)
                    dve.wait_ge(za_max, c + 1)
                    dve.scalar_tensor_tensor(out=sm[:, 0, 0:4], in0=sm[:, 0, 4:8], scalar=-SCALE,
                                             in1=nsink_c[:], op0=ALU.mult, op1=ALU.min).then_inc(za_bias, 1)
                    dve.wait_ge(za_bias, 2 * c + 1)
                    dve.tensor_tensor(sm[:, 1, 0:4], sm[:, 0, 0:4], sink_c[:], ALU.add).then_inc(za_bias, 1)
                if c >= 3:
                    i = c - 3
                    dve.wait_ge(oa_done, i + 1)
                    bank = 7 if i % 2 == 0 else 4
                    dve.tensor_copy(o_t[:, 0:4, CHUNK * i:CHUNK * (i + 1)],
                                    ps[:, bank, 0:4 * CHUNK].rearrange("p (a t) -> p a t", t=CHUNK)
                                    ).then_inc(oa_free, 1)
            def gate_a_product(i):
                dve.wait_ge(ga_sig, i + 1)
                sg = beta[:, i % 2, 0:SEQ]
                dve.tensor_tensor(sg, sg, o_t[:, 4 + i, :], ALU.mult).then_inc(ga_mul, 1)
                dve.wait_ge(ga_mul, i + 1)
                if i == 0:
                    dve.wait_ge(oa_free, NCHUNK)
                dve.tensor_tensor(o_t[:, i, :], o_t[:, i, :], sg, ALU.mult).then_inc(ga_set, 1)

            for i in range(4):
                gate_a_product(i)
            dve.memset(stick_a[:, 0:1], 1.0).then_inc(stick_ones, 1)
            dve.memset(stick_b[:, 0:1], 1.0).then_inc(stick_ones, 1)

            def parts(k):
                h, tb, n1, tb2, n2 = step(k)
                return (stick_a, 0, n1), (stick_b, n1, n2)

            def scan(p, k, q):
                i = 8 * p + k
                stick, at, m = parts(k)[q]
                kp = keep[:, i % 2, at:at + m]
                dve.wait_ge(kept, 2 * i + q + 1)
                if i > 0:
                    dve.wait_ge(w_ready, 2 * (i - 1) + q + 1)
                dve.tensor_tensor_scan(stick[:, 1:m + 1], kp, kp, 1.0,
                                       ALU.mult, ALU.bypass).then_inc(scanned, 1)

            def break_sticks(p, k):
                i = 8 * p + k
                for q, (stick, at, m) in enumerate(parts(k)):
                    bt = beta[:, i % 2, at:at + m]
                    dve.wait_ge(scanned, 2 * i + q + 1)
                    dve.tensor_tensor(bt, bt, stick[:, 0:m], ALU.mult).then_inc(w_ready, 1)

            def turned_lo(p, k, groups):
                for g in groups:
                    i = T_PAIR * p + 2 + T_GROUPS * k + g
                    nb = 4 if g < 2 else 1
                    dve.wait_ge(tb_hi, i + 1)
                    dve.tensor_tensor(w_t[:, 4 * g:4 * g + nb, 1, :],
                                      ps[:, 5 + i % 2, 0:P * nb].rearrange("p (a t) -> p a t", t=P),
                                      w_t[:, 4 * g:4 * g + nb, 0, :].bitcast(F32),
                                      ALU.subtract).then_inc(tb_free, 1)

            def values_lo(p):
                for g in range(2):
                    i = T_PAIR * p + g
                    dve.wait_ge(tb_hi, i + 1)
                    dve.tensor_tensor(v_n[:, 4 * g:4 * g + 4, :, 1, :],
                                      ps[:, 5 + i % 2, :].rearrange("p (a h d) -> p a h d", h=2, d=HD),
                                      v_n[:, 4 * g:4 * g + 4, :, 0, :].bitcast(F32),
                                      ALU.subtract).then_inc(tb_free, 1)

            def sum_out(p, k):
                h, i = k % 2, 8 * p + k
                r = slice(HD * h, HD * h + HD)
                dve.wait_ge(o_copied, i + 1)
                dve.tensor_tensor(o_part[r, :], ps[r, 7, :], o_part[r, :], ALU.add).then_inc(o_free, 1)

            def step_low(p, k):
                if 1 <= k <= 8:
                    scan(p, k - 1, 0)
                if k >= 3:
                    turned_lo(p, k - 3, (2,))
                if 1 <= k <= 8:
                    scan(p, k - 1, 1)
                    break_sticks(p, k - 1)
                if k >= 2:
                    turned_lo(p, k - 2, (0, 1))
                if k >= 3:
                    sum_out(p, k - 3)

            dve.wait_ge(stick_ones, 2)
            for p in range(PAIRS):
                n = LOOP_B + 4 * p
                last = p == PAIRS - 1
                if p > 0:
                    step_low(p - 1, 8)
                head_lo(p, n, 0, ks, True)
                if p > 0:
                    step_low(p - 1, 9)
                head_lo(p, n, 1, ks, True)
                if p > 0:
                    turned_lo(p - 1, 7, (2,))
                    sum_out(p - 1, 7)
                values_lo(p)
                head_lo(p, n + 1, 0, qs, False)
                head_lo(p, n + 1, 1, qs, False)
                for k in range(8):
                    step_low(p, k)
            step_low(PAIRS - 1, 8)
            def branch_lo(k):
                dve.wait_ge(oh_done, k + 1)
                if k == KT - 1:
                    dve.wait_ge(o_set, 16 * PAIRS)
                dve.tensor_tensor(r_lo[:, k, :], o_t[:, k, :], r_hi[:, k, :].bitcast(F32),
                                  ALU.subtract).then_inc(ol_done, 1)

            turned_lo(PAIRS - 1, 6, (2,))
            for k in range(EARLY):
                branch_lo(k)
            turned_lo(PAIRS - 1, 7, (0, 1))
            sum_out(PAIRS - 1, 6)
            turned_lo(PAIRS - 1, 7, (2,))
            sum_out(PAIRS - 1, 7)
            for k in range(EARLY, KT):
                branch_lo(k)

            def merge(j):
                dve.wait_ge(up_done, j + 1)
                dve.wait_ge(mg_sig, 4 * j + 4)
                for h in range(2):
                    sig_a, sig_b = sig_m[:, 2 * (j % 2) + h, :], sig_m[:, 4 + h, :]
                    dve.tensor_tensor(sig_a, sig_a, ps[:, 2 + h, :], ALU.mult).then_inc(ya_mul, 1)
                    dve.tensor_tensor(sig_b, sig_b, ps[:, 4 + h, :], ALU.mult).then_inc(yb_mul, 1)
                    dve.wait_ge(ya_mul, 2 * j + h + 1)
                    dve.wait_ge(yb_mul, 2 * j + h + 1)
                    dve.tensor_tensor(o_t[:, j, half(h)], sig_a, sig_b, ALU.add).then_inc(m_set, 1)

            def merged_lo(k):
                dve.wait_ge(mh_done, k + 1)
                dve.tensor_tensor(x_lo[:, k, :], o_t[:, k, :], x_hi[:, k, :].bitcast(F32),
                                  ALU.subtract).then_inc(ml_done, 1)

            def w_out_lo(k):
                dve.wait_ge(wo_hi, k)
                dve.tensor_tensor(r_lo[:, k, :], raw[:, (W_OUT + k) % 2, :], r_hi[:, k, :].bitcast(F32),
                                  ALU.subtract).then_inc(wo_lo, 1)

            for j in range(KT - 1):
                merge(j)
            merged_lo(0)
            merged_lo(1)
            merge(KT - 1)
            for k in range(1, KT):
                w_out_lo(k)
                if k + 1 < KT:
                    merged_lo(k + 1)
            dve.wait_ge(ml_done, KT)
            dve.wait_ge(ln_in, 32)
            chain = 0
            for s in range(SB):
                r = o_t[:, s % 2, :]
                y = o_t[:, 2 + s % 2, :]
                st = small[:, s % 2, :]
                bn = small[:, 4 + 2 * (s % 2):6 + 2 * (s % 2), 0:6]
                dve.wait_ge(xn_in[s % 2], 16 * (s // 2 + 1))
                for h in range(2):
                    dve.wait_ge(r_psum, 2 * s + h + 1)
                    if s >= 2:
                        dve.wait_ge(ln_gain, 2 * (s - 2) + h + 1)
                    dve.scalar_tensor_tensor(out=r[:, half(h)], in0=raw[:, s % 2, half(h)], scalar=ALPHA,
                                             in1=ps[:, out_bank(s, h), :], op0=ALU.mult,
                                             op1=ALU.add).then_inc(r_set, 1)
                    dve.wait_ge(r_set, 2 * s + h + 1)
                    dve.bn_stats(bn[:, h, :], r[:, half(h)]).then_inc(ln_chain, 1)
                chain += 2
                dve.wait_ge(ln_chain, chain)
                dve.bn_aggr(st[:, 0:2], bn).then_inc(ln_var, 1)
                if s == SB - 1:
                    break
                dve.wait_ge(ln_std, s + 1)
                dve.reciprocal(st[:, 3:4], st[:, 2:3]).then_inc(ln_chain, 1)
                chain += 1
                dve.wait_ge(ln_chain, chain)
                dve.scalar_tensor_tensor(out=st[:, 4:5], in0=st[:, 0:1], scalar=-1.0, in1=st[:, 3:4],
                                         op0=ALU.mult, op1=ALU.mult).then_inc(ln_nb, 1)
            dve.wait_ge(out_done[s % 2], 32 * (s // 2))
            dve.wait_ge(ln_var, SB)
            for h in range(2):
                dve.scalar_tensor_tensor(out=y[:, half(h)], in0=r[:, half(h)], scalar=st[:, 0:1],
                                         in1=g_bc[:, half(h)], op0=ALU.subtract,
                                         op1=ALU.mult).then_inc(ln_chain, 1)
                if h == 0:
                    dve.wait_ge(ln_std, SB)
                    dve.reciprocal(st[:, 3:4], st[:, 2:3]).then_inc(ln_chain, 1)
                    chain += 1
                chain += 1
                dve.wait_ge(ln_chain, chain)
                dve.scalar_tensor_tensor(out=y[:, half(h)], in0=y[:, half(h)], scalar=st[:, 3:4],
                                         in1=b_bc[:, half(h)], op0=ALU.mult, op1=ALU.add).then_inc(ln_last, 1)

        @block.tensor
        def _(pe):
            def chunk(n, q, use=None):
                use = n if use is None else use
                h, s = q // 2, n % 2
                bank = 2 + h if n == V_A else h
                if n <= V_A and q == 0:
                    pe.wait_ge(first_lo, n + 1)
                elif q == 0 or n <= V_A:
                    pe.wait_ge(lo_done, n + 1)
                if q % 2 == 0 and n != V_A:
                    if use > USE_U:
                        pe.wait_ge(mg_sig, 2 * (use - 1 - USE_U) + h + 1)
                    elif use > 0:
                        pe.wait_ge(bank_free[h], use)
                for k in range(4 * (q % 2), 4 * (q % 2) + 4):
                    if n == 0:
                        pe.wait_ge(x_lo_done, KT * h + k + 1)
                    wk = slice(P * k, P * (k + 1))
                    xs = slice(HALF * h, HALF * (h + 1))
                    last = mma3(pe, ps[:, bank, :], w_hi[:, s, wk], w_lo[:, s, wk], x_hi[:, k, xs],
                                x_lo[:, k, xs], k == 0, k == KT - 1)
                if q % 2 == 1:
                    last.then_inc(half_done, 1)

            def t_bank(i):
                if i >= 2:
                    pe.wait_ge(tp_free, i - 1)
                return ps[:, 5 + i % 2, :]

            pe.wait_ge(masks, 2)
            for _ in range(WARM_UP):
                pe.transpose(ps[:, 7, 0:P], ident[:], ident[:])

            for h in range(2):
                for n in (K_A, V_A):
                    chunk(n, 2 * h)
                    chunk(n, 2 * h + 1)
            for n in range(Q_A, GATE_A):
                for q in range(4):
                    chunk(n, q)
                if n == Q_A:
                    pe.wait_ge(masks, 2)
                    for h in range(2):
                        pe.wait_ge(bank_free[h], V_A + 1)
                if n >= Q_A:
                    i = n - Q_A
                    bank = t_bank(i)
                    for b_ in range(4):
                        c = 4 * i + b_
                        keys = P if c < NCHUNK - 1 else CHUNK
                        last = pe.transpose(bank[0:keys, P * b_:P * (b_ + 1)],
                                            v_t[:, CHUNK * c:CHUNK * c + keys], ident[:])
                    last.then_inc(tp_done, 1)

            def fill(i):
                chunk(GATE_A + i // 4, i % 4)

            fill(0)
            fill(1)
            for c in range(NCHUNK + 3):
                if 2 <= c < NCHUNK + 2:
                    i = c - 2
                    keys = P if i < NCHUNK - 1 else CHUNK
                    pe.wait_ge(za_p, i + 1)
                    bank = t_bank(4 + i)
                    for cb in range(4):
                        last = pe.transpose(bank[0:keys, P * cb:P * (cb + 1)],
                                            prob[:, i % 3, P * cb:P * cb + keys], ident[:])
                    last.then_inc(tp_done, 1)
                fill(c + 2)
                if c < NCHUNK:
                    if c == 0:
                        pe.wait_ge(k_dup, 64)
                        pe.wait_ge(q_split, 16)
                    if c >= 2:
                        pe.wait_ge(za_exp, 5 * (c - 1))
                    keys = P if c < NCHUNK - 1 else CHUNK
                    for g in range(2):
                        for pr in range(2):
                            cb = 2 * g + pr
                            o = ps[:, 2 + c % 2, P * cb:P * cb + keys]
                            q_ = qa[:, g, c, 2 * pr:2 * pr + 2, :].rearrange("p a t -> p (a t)")
                            for part in range(2):
                                last = pe.matmul(o, q_, ka[:, part, g, CHUNK * c:CHUNK * c + keys],
                                                 start=part == 0, stop=part == 1)
                    last.then_inc(za_done, 1)
                if c >= 3:
                    i = c - 3
                    pe.wait_ge(tp_free, 4 + i + 1)
                    if i >= 2:
                        pe.wait_ge(oa_free, i - 1)
                    keys = P if i < NCHUNK - 1 else CHUNK
                    bank = 7 if i % 2 == 0 else 4
                    for g in range(2):
                        last = pe.matmul(ps[HD * g:HD * g + HD, bank, 0:4 * CHUNK],
                                         v_win[0:keys, i, HD * g:HD * g + HD],
                                         prob_t[0:keys, i % 2, 2 * P * g:2 * P * (g + 1)],
                                         start=True, stop=True)
                    last.then_inc(oa_done, 1)

            for q in range(1, 4):
                chunk(GATE_B0, q)

            def tb_bank(i):
                if i >= 2:
                    pe.wait_ge(tb_free, i - 1)
                else:
                    pe.wait_ge(tp_free, 4 + NCHUNK)
                return ps[:, 5 + i % 2, :]

            def turn(p, k, groups):
                i = 8 * p + k
                for g in groups:
                    pe.wait_ge(w_ready, 2 * (i + 1))
                    bank = tb_bank(T_PAIR * p + 2 + T_GROUPS * k + g)
                    for b_ in range(4 * g, min(4 * g + 4, SB + 1)):
                        at = P * (b_ % 4)
                        last = pe.transpose(bank[:, at:at + P], beta[:, i % 2, P * b_:P * (b_ + 1)], ident[:])
                    last.then_inc(tb_done, 1)

            def scores(p, k):
                h, tb, n1, tb2, n2 = step(k)
                i = 8 * p + k
                if i > 0:
                    pe.wait_ge(za_free, i)
                    pe.wait_ge(zb_free, i)
                for z, t, width in ((z_big, tb, n1), (z_small, tb2, n2)):
                    for at in range(0, width, HALF):
                        m = min(HALF, width - at)
                        for part in range(2):
                            last = pe.matmul(z[:, at:at + m], qs[:, h, P * t:P * (t + 1)],
                                             ks[:, part, h, P * t + at:P * t + at + m],
                                             start=part == 0, stop=part == 1)
                last.then_inc(z_done, 1)

            def values(p, k, blocks):
                h, tb, n1, tb2, n2 = step(k)
                i = 8 * p + k
                if i >= 1:
                    pe.wait_ge(o_free, i)
                nb1 = n1 // P
                for b_ in blocks:
                    if b_ % 4 == 0:
                        pe.wait_ge(tb_free, T_PAIR * p + 2 + T_GROUPS * k + b_ // 4 + 1)
                    small_b = b_ >= nb1
                    kb = tb2 + b_ - nb1 if small_b else tb + b_
                    last = pe.matmul(ps[:, 7, 2 * P * small_b:2 * P * (small_b + 1)],
                                     v_n[:, kb, h, :, :].rearrange("p a d -> p (a d)"),
                                     w_t[:, b_, :, :].rearrange("p a t -> p (a t)"),
                                     start=b_ in (0, nb1), stop=b_ in (nb1 - 1, SB))
                if SB in blocks:
                    last.then_inc(o_done, 1)

            FIRST, LAST = range(SB), (SB,)

            def last_steps(p, n, use):
                turn(p, 6, (0, 1))
                values(p, 5, LAST)
                chunk(n, 1, use)
                turn(p, 6, (2,))
                chunk(n, 2, use)
                values(p, 6, FIRST)
                turn(p, 7, (0, 1))
                values(p, 6, LAST)
                chunk(n, 3, use)
                turn(p, 7, (2,))
                values(p, 7, FIRST)

            for p in range(PAIRS):
                n = LOOP_B + 4 * p
                if p == 0:
                    for q in range(4):
                        chunk(n, q)
                else:
                    last_steps(p - 1, n, n)
                chunk(n + 1, 0)
                if p > 0:
                    values(p - 1, 7, LAST)
                for h in range(2):
                    pe.wait_ge(bank_free[h], V_B0 + 4 * p + 1)
                for g in range(2):
                    bank = tb_bank(T_PAIR * p + g)
                    for b_ in range(4 * g, 4 * g + 4):
                        last = pe.transpose(bank[:, P * (b_ % 4):P * (b_ % 4) + P], v_t[:, P * b_:P * (b_ + 1)],
                                            ident[:])
                    last.then_inc(tb_done, 1)
                for q in range(1, 4):
                    chunk(n + 1, q)
                for k in range(8):
                    if k >= 2:
                        turn(p, k - 2, (0, 1))
                    if k >= 3:
                        values(p, k - 3, LAST)
                    if k >= 2:
                        scores(p, k)
                    if k == 7 and p == PAIRS - 1:
                        chunk(n + 4, 0, USE_U + 2)
                    elif k < 2:
                        chunk(n + 2, k)
                    else:
                        chunk(n + 2 + (k + 1) // 4, (k + 1) % 4)
                    if k == 0:
                        pe.wait_ge(k_dup, 64 * (p + 2))
                        for h in range(2):
                            pe.wait_ge(bank_free[h], n + 2)
                    if k >= 2:
                        turn(p, k - 2, (2,))
                    if k < 2:
                        scores(p, k)
                    if k == 1:
                        chunk(n + 2, 2)
                    if k >= 2:
                        values(p, k - 2, FIRST)

            def up(j):
                n = up_tile(j)
                pe.wait_ge(lo_done, n + 1)
                if j > 0:
                    pe.wait_ge(yb_mul, 2 * j)
                s = n % 2
                for ab in range(2):
                    for k in range(4):
                        kk = 4 * ab + k
                        if j == 0:
                            pe.wait_ge(ol_done, kk + 1)
                        for h in range(2):
                            wk = slice(P * kk, P * (kk + 1))
                            xs = slice(HALF * h, HALF * (h + 1))
                            last = mma3(pe, ps[:, 2 + 2 * ab + h, :], w_hi[:, s, wk], w_lo[:, s, wk],
                                        r_hi[:, kk, xs], r_lo[:, kk, xs], k == 0, k == 3)
                last.then_inc(up_done, 1)

            for j in range(1, KT):
                n = merge_tile(j, 0)
                if j == 1:
                    last_steps(PAIRS - 1, n, USE_U + 2)
                    values(PAIRS - 1, 7, LAST)
                else:
                    for q in range(4):
                        chunk(n, q, USE_U + 2 * j)
                up(j - 1)
                for q in range(4):
                    chunk(merge_tile(j, 1), q, USE_U + 2 * j + 1)
            up(KT - 1)

            def w_out_parts(k, h):
                ws = slice(HALF * h, HALF * (h + 1))
                if k == 0:
                    return w_hi[:, W_OUT % 2, ws], w_lo[:, W_OUT % 2, ws]
                return r_hi[:, k, ws], r_lo[:, k, ws]

            for k in range(KT):
                pe.wait_ge(ml_done, k + 1)
                if k == 0:
                    pe.wait_ge(lo_done, W_OUT + 1)
                else:
                    pe.wait_ge(wo_lo, k)
                for s in range(4):
                    if k == 0 and s == 0:
                        pe.wait_ge(mg_sig, 4 * KT)
                    for h in range(2):
                        if k == 0 and s == 2:
                            pe.wait_ge(ya_mul, 2 * (KT - 1) + h + 1)
                        if k == 0 and s == 3:
                            pe.wait_ge(yb_mul, 2 * (KT - 1) + h + 1)
                        xs = slice(P * s, P * (s + 1))
                        last = mma3(pe, ps[:, out_bank(s, h), :], x_hi[:, k, xs], x_lo[:, k, xs],
                                    *w_out_parts(k, h), k == 0, k == KT - 1)
                        if k == KT - 1:
                            last.then_inc(r_psum, 1)
            for s in range(4, SB):
                for h in range(2):
                    pe.wait_ge(r_set, 2 * (s - 4) + h + 1)
                    for k in range(KT):
                        xs = slice(P * s, P * (s + 1))
                        last = mma3(pe, ps[:, out_bank(s, h), :], x_hi[:, k, xs], x_lo[:, k, xs],
                                    *w_out_parts(k, h), k == 0, k == KT - 1)
                    last.then_inc(r_psum, 1)


def columns():
    at = np.cumsum([0, 512, 128, 128, 512, 512, 512, 512, 512, D, D])
    q_a, k_a, v_a, gate_a, q_b, k_b, v_b, gate_b, mg_a, mg_b = at[:-1]
    tile = np.arange(P)

    def heads(base, i):
        return np.concatenate([base + HD * (GROUP * g + i) + np.arange(HD) for g in range(2)])

    order = {K_A: k_a + tile, V_A: v_a + tile}
    for i in range(4):
        order[Q_A + i] = heads(q_a, i)
        order[GATE_A + i] = heads(gate_a, i)
    for p in range(PAIRS):
        order[V_B0 if p == 0 else LOOP_B + 4 * p - 2] = v_b + P * p + tile
        order[GATE_B0 if p == 0 else LOOP_B + 4 * p - 1] = gate_b + P * p + tile
        order[LOOP_B + 4 * p] = k_b + P * p + tile
        order[LOOP_B + 4 * p + 1] = q_b + P * p + tile
    for j in range(KT):
        order[merge_tile(j, 0)] = mg_a + P * j + tile
        order[merge_tile(j, 1)] = mg_b + P * j + tile
    return order


def kernel(x, w_in, b_in, sinks, w_up_a, w_up_b, w_out, ln_g, ln_b):
    import concourse.bacc as bacc
    from concourse.bass_utils import run_bass_kernel_spmd

    x, w_in, b_in, sinks, w_up_a, w_up_b, w_out, ln_g, ln_b = (
        np.asarray(t)[0] for t in (x, w_in, b_in, sinks, w_up_a, w_up_b, w_out, ln_g, ln_b))
    backwards = x[::-1]
    w = np.empty((N_TILES, P, D), x.dtype)
    bias = np.zeros((P, W_OUT), x.dtype)
    for n, cols in columns().items():
        w[n] = w_in[:, cols].reshape(KT, P, P).transpose(1, 0, 2).reshape(P, D)
        bias[:, n] = b_in[cols]
    up_rows = np.concatenate([HD * (GROUP * g + i) + np.arange(HD) for i in range(4) for g in range(2)])
    up = np.concatenate([w_up_a[up_rows], w_up_b])
    for j in range(KT):
        w[up_tile(j)] = up[:, P * j:P * (j + 1)].reshape(KT, P, P).transpose(1, 0, 2).reshape(P, D)
        w[W_OUT + j] = w_out[P * j:P * (j + 1)]
    sink_rows = np.repeat(sinks.reshape(2, 2, 2).transpose(2, 0, 1).reshape(2, GROUP), CHUNK, axis=0)
    half = HD // 2
    freq = np.float32(10000.0) ** (-np.arange(half, dtype=np.float32) / np.float32(half))
    angle = (freq[:, None] * np.arange(SEQ, dtype=np.float32)[None, ::-1]).astype(np.float64)
    cos = np.tile(np.cos(angle), (4, 1)).astype(np.float32)
    sin = np.tile(np.concatenate([-np.sin(angle), np.sin(angle)]), (2, 1)).astype(np.float32)
    arrays = {
        "xt": np.ascontiguousarray(backwards.T).reshape(KT, P, SEQ),
        "xn": np.ascontiguousarray(backwards).reshape(SB, P, D),
        "w": w, "bias": bias, "cos": cos, "sin": sin, "sinks": np.ascontiguousarray(sink_rows),
        "ln_g": np.ascontiguousarray(np.broadcast_to(ln_g, (P, D))),
        "ln_b": np.ascontiguousarray(np.broadcast_to(ln_b, (P, D))),
    }
    nc = bacc.Bacc("TRN2", target_bir_lowering=False, num_devices=1)
    args = [nc.dram_tensor(f"in_{k}", a.shape, mybir.dt.from_np(a.dtype), kind="ExternalInput").ap()
            for k, a in arrays.items()]
    out = nc.dram_tensor("out_0", (SB, P, D), F32, kind="ExternalOutput").ap()
    build(nc, *args, out)
    r = run_bass_kernel_spmd(nc, [{f"in_{k}": a for k, a in arrays.items()}], core_ids=[0])
    return r.results[0]["out_0"].reshape(SEQ, D)[::-1].reshape(1, SEQ, D)
```
